# Optimizing a Trainium2 kernel written in Bass

```python
import jax, jax.numpy as jnp
from jax import lax
import numpy as np
import math

D_MODEL = 1024
BATCH = 1
SEQ = 256
DEPTH = 2

HEAD_DIM = 64
EPS = 1e-6
N_BRANCH = 3
CONV_WIDTH = D_MODEL
CONV_KERNEL = 31
RET_HEADS = 4
RET_QK_DIM = D_MODEL // RET_HEADS
RET_V_DIM = 2 * RET_QK_DIM
RET_CHUNK = 128
RET_THETA = 10000.0
ATTN_HEADS = D_MODEL // HEAD_DIM
ATTN_KV_HEADS = 4
ATTN_WINDOW = 128
ATTN_BLOCK = 128
ROPE_THETA = 500000.0
ROPE_DIM = HEAD_DIM // 4

IN_SPLITS = (
    2 * CONV_WIDTH,
    CONV_WIDTH,
    RET_HEADS * RET_QK_DIM,
    RET_HEADS * RET_QK_DIM,
    RET_HEADS * RET_V_DIM,
    RET_HEADS * RET_V_DIM,
    ATTN_HEADS * HEAD_DIM,
    ATTN_KV_HEADS * HEAD_DIM,
    ATTN_KV_HEADS * HEAD_DIM,
    ATTN_HEADS * HEAD_DIM,
    N_BRANCH * D_MODEL,
)
IN_WIDTH = sum(IN_SPLITS)


def rms_norm(x, g):
    xf = x.astype(jnp.float32)
    y = xf * lax.rsqrt(jnp.mean(xf * xf, axis=-1, keepdims=True) + EPS) * g.astype(jnp.float32)
    return y.astype(x.dtype)

def rotary(x, positions, theta, rot_dim):
    half = rot_dim // 2
    inv_freq = theta ** (-jnp.arange(half, dtype=jnp.float32) / half)
    ang = positions.astype(jnp.float32)[:, None] * inv_freq[None, :]
    cos = jnp.cos(ang)[:, None, :]
    sin = jnp.sin(ang)[:, None, :]
    xf = x.astype(jnp.float32)
    x1 = xf[..., :half]
    x2 = xf[..., half:rot_dim]
    out = jnp.concatenate([x1 * cos - x2 * sin, x2 * cos + x1 * sin, xf[..., rot_dim:]], axis=-1)
    return out.astype(x.dtype)

def conv_module(u_glu, gate, dw, db, ln_g, ln_b):
    a, b = jnp.split(u_glu, 2, axis=-1)
    v = a * jax.nn.sigmoid(b)
    y = lax.conv_general_dilated(
        v, dw[:, None, :].astype(v.dtype), window_strides=(1,),
        padding=[(CONV_KERNEL // 2, CONV_KERNEL // 2)],
        dimension_numbers=('NWC', 'WIO', 'NWC'),
        feature_group_count=CONV_WIDTH) + db.astype(v.dtype)
    yf = y.astype(jnp.float32)
    mu = jnp.mean(yf, axis=-1, keepdims=True)
    var = jnp.mean(jnp.square(yf - mu), axis=-1, keepdims=True)
    yf = (yf - mu) * lax.rsqrt(var + EPS) * ln_g.astype(jnp.float32) + ln_b.astype(jnp.float32)
    y = jax.nn.silu(yf).astype(v.dtype)
    return y * jax.nn.silu(gate)

def retention_one_direction(q, k, v, log_gamma, inclusive):
    B, H, S, dk = q.shape
    dv = v.shape[-1]
    C = RET_CHUNK
    n = S // C
    qc = q.reshape(B, H, n, C, dk)
    kc = k.reshape(B, H, n, C, dk)
    vc = v.reshape(B, H, n, C, dv)
    idx = jnp.arange(C, dtype=jnp.float32)
    diff = idx[:, None] - idx[None, :]
    mask = (diff >= 0) if inclusive else (diff > 0)
    lg = log_gamma[:, None, None]
    decay_inner = jnp.where(mask[None], jnp.exp(lg * jnp.where(mask, diff, 0.0)[None]), 0.0)
    scores = jnp.einsum('bhnid,bhnjd->bhnij', qc, kc) * decay_inner[None, :, None]
    inner = jnp.einsum('bhnij,bhnjv->bhniv', scores, vc)
    q_decay = jnp.exp(log_gamma[:, None] * (idx[None, :] + 1.0))[None, :, :, None]
    k_decay = jnp.exp(log_gamma[:, None] * (C - 1.0 - idx[None, :]))[None, :, :, None]
    chunk_decay = jnp.exp(log_gamma * C)[None, :, None, None]

    def step(state, xs):
        q_t, k_t, v_t = xs
        cross = jnp.einsum('bhcd,bhdv->bhcv', q_t * q_decay, state)
        state = chunk_decay * state + jnp.einsum('bhcd,bhcv->bhdv', k_t * k_decay, v_t)
        return state, cross

    state0 = jnp.zeros((B, H, dk, dv), jnp.float32)
    xs = (jnp.moveaxis(qc, 2, 0), jnp.moveaxis(kc, 2, 0), jnp.moveaxis(vc, 2, 0))
    _, cross = lax.scan(step, state0, xs)
    out = inner + jnp.moveaxis(cross, 0, 2)
    return out.reshape(B, H, S, dv)

def retention_branch(q, k, v, gate, ret_decay, positions):
    B, S, _ = q.shape
    q = rotary(q.reshape(B, S, RET_HEADS, RET_QK_DIM), positions, RET_THETA, RET_QK_DIM)
    k = rotary(k.reshape(B, S, RET_HEADS, RET_QK_DIM), positions, RET_THETA, RET_QK_DIM)
    qf = jnp.transpose(q, (0, 2, 1, 3)).astype(jnp.float32)
    kf = jnp.transpose(k, (0, 2, 1, 3)).astype(jnp.float32) * (RET_QK_DIM ** -0.5)
    vf = jnp.transpose(v.reshape(B, S, RET_HEADS, RET_V_DIM), (0, 2, 1, 3)).astype(jnp.float32)
    log_gamma = -jnp.exp(ret_decay.astype(jnp.float32))
    fwd = retention_one_direction(qf, kf, vf, log_gamma[0], True)
    bwd = retention_one_direction(qf[:, :, ::-1], kf[:, :, ::-1], vf[:, :, ::-1], log_gamma[1], False)[:, :, ::-1]
    o = fwd + bwd
    mu = jnp.mean(o, axis=-1, keepdims=True)
    var = jnp.mean(jnp.square(o - mu), axis=-1, keepdims=True)
    o = (o - mu) * lax.rsqrt(var + EPS)
    o = jnp.transpose(o, (0, 2, 1, 3)).reshape(B, S, RET_HEADS * RET_V_DIM).astype(gate.dtype)
    return o * jax.nn.silu(gate)

def window_attention_branch(q, k, v, gate, q_norm_g, k_norm_g, sink, positions):
    B, S, _ = q.shape
    G = ATTN_HEADS // ATTN_KV_HEADS
    T = ATTN_BLOCK
    nb = S // T
    q = rms_norm(q.reshape(B, S, ATTN_HEADS, HEAD_DIM), q_norm_g)
    k = rms_norm(k.reshape(B, S, ATTN_KV_HEADS, HEAD_DIM), k_norm_g)
    q = rotary(q, positions, ROPE_THETA, ROPE_DIM)
    k = rotary(k, positions, ROPE_THETA, ROPE_DIM)
    v = v.reshape(B, S, ATTN_KV_HEADS, HEAD_DIM)
    qb = q.reshape(B, nb, T, ATTN_KV_HEADS, G, HEAD_DIM).astype(jnp.float32)
    pad = ((0, 0), (T, T), (0, 0), (0, 0))
    kb = jnp.pad(k, pad).reshape(B, nb + 2, T, ATTN_KV_HEADS, HEAD_DIM)
    vb = jnp.pad(v, pad).reshape(B, nb + 2, T, ATTN_KV_HEADS, HEAD_DIM)
    kwin = jnp.concatenate([kb[:, :-2], kb[:, 1:-1], kb[:, 2:]], axis=2).astype(jnp.float32)
    vwin = jnp.concatenate([vb[:, :-2], vb[:, 1:-1], vb[:, 2:]], axis=2).astype(jnp.float32)
    s = jnp.einsum('bnqhgd,bnjhd->bhgnqj', qb, kwin) * (HEAD_DIM ** -0.5)
    blk = jnp.arange(nb)[:, None, None]
    qpos = blk * T + jnp.arange(T)[None, :, None]
    kpos = (blk - 1) * T + jnp.arange(3 * T)[None, None, :]
    valid = (jnp.abs(kpos - qpos) <= ATTN_WINDOW) & (kpos >= 0) & (kpos < S)
    s = jnp.where(valid, s, -1e30)
    sink_l = sink.astype(jnp.float32).reshape(ATTN_KV_HEADS, G, 1, 1, 1)
    m = jnp.maximum(jnp.max(s, axis=-1, keepdims=True), sink_l)
    p = jnp.exp(s - m)
    p = p / (jnp.sum(p, axis=-1, keepdims=True) + jnp.exp(sink_l - m))
    o = jnp.einsum('bhgnqj,bnjhd->bnqhgd', p, vwin)
    o = o.reshape(B, S, ATTN_HEADS * HEAD_DIM).astype(gate.dtype)
    return o * jax.nn.silu(gate)

def hybrid_layer(x, positions, norm_g, w_in, b_gate, conv_dw, conv_b, conv_ln_g, conv_ln_b,
                 ret_decay, q_norm_g, k_norm_g, attn_sink, w_conv_out, w_ret_out, w_attn_out, w_out):
    B, S, D = x.shape
    h = rms_norm(x, norm_g)
    z = h @ w_in
    offsets = np.cumsum(IN_SPLITS)[:-1].tolist()
    (c_glu, c_gate, r_q, r_k, r_v, r_gate, a_q, a_k, a_v, a_gate, g_logit) = jnp.split(z, offsets, axis=-1)
    y_conv = conv_module(c_glu, c_gate, conv_dw, conv_b, conv_ln_g, conv_ln_b) @ w_conv_out
    y_ret = retention_branch(r_q, r_k, r_v, r_gate, ret_decay, positions) @ w_ret_out
    y_attn = window_attention_branch(a_q, a_k, a_v, a_gate, q_norm_g, k_norm_g, attn_sink, positions) @ w_attn_out
    g = jax.nn.sigmoid(g_logit + b_gate).reshape(B, S, N_BRANCH, D)
    merged = g[:, :, 0] * y_conv + g[:, :, 1] * y_ret + g[:, :, 2] * y_attn
    return x + merged @ w_out

def first_inputs(seed: int = 0) -> dict:
    key = jax.random.key(seed)
    ks = jax.random.split(key, 18)
    nrm = jax.random.normal
    f32 = jnp.float32
    ret_base = jnp.log(-jnp.log1p(-(2.0 ** (-5.0 - jnp.arange(RET_HEADS, dtype=f32)))))
    return {
        'x': nrm(ks[0], (BATCH, SEQ, D_MODEL), f32),
        'norm_g': 1.0 + 0.02 * nrm(ks[1], (DEPTH, D_MODEL), f32),
        'w_in': nrm(ks[2], (DEPTH, D_MODEL, IN_WIDTH), f32) * D_MODEL ** -0.5,
        'b_gate': 0.1 * nrm(ks[3], (DEPTH, N_BRANCH * D_MODEL), f32),
        'conv_dw': nrm(ks[4], (DEPTH, CONV_KERNEL, CONV_WIDTH), f32) * CONV_KERNEL ** -0.5,
        'conv_b': 0.02 * nrm(ks[5], (DEPTH, CONV_WIDTH), f32),
        'conv_ln_g': 1.0 + 0.02 * nrm(ks[6], (DEPTH, CONV_WIDTH), f32),
        'conv_ln_b': 0.02 * nrm(ks[7], (DEPTH, CONV_WIDTH), f32),
        'ret_decay': ret_base + 0.05 * nrm(ks[8], (DEPTH, 2, RET_HEADS), f32),
        'q_norm_g': 1.0 + 0.02 * nrm(ks[9], (DEPTH, HEAD_DIM), f32),
        'k_norm_g': 1.0 + 0.02 * nrm(ks[10], (DEPTH, HEAD_DIM), f32),
        'attn_sink': 0.5 * nrm(ks[11], (DEPTH, ATTN_HEADS), f32),
        'w_conv_out': nrm(ks[12], (DEPTH, CONV_WIDTH, D_MODEL), f32) * CONV_WIDTH ** -0.5,
        'w_ret_out': nrm(ks[13], (DEPTH, RET_HEADS * RET_V_DIM, D_MODEL), f32) * (RET_HEADS * RET_V_DIM) ** -0.5,
        'w_attn_out': nrm(ks[14], (DEPTH, ATTN_HEADS * HEAD_DIM, D_MODEL), f32) * (ATTN_HEADS * HEAD_DIM) ** -0.5,
        'w_out': nrm(ks[15], (DEPTH, D_MODEL, D_MODEL), f32) * D_MODEL ** -0.5,
    }

def first_block(x, norm_g, w_in, b_gate, conv_dw, conv_b, conv_ln_g, conv_ln_b, ret_decay,
              q_norm_g, k_norm_g, attn_sink, w_conv_out, w_ret_out, w_attn_out, w_out):
    positions = jnp.arange(x.shape[1], dtype=jnp.int32)
    for l in range(DEPTH):
        x = hybrid_layer(x, positions, norm_g[l], w_in[l], b_gate[l], conv_dw[l], conv_b[l],
                         conv_ln_g[l], conv_ln_b[l], ret_decay[l], q_norm_g[l], k_norm_g[l],
                         attn_sink[l], w_conv_out[l], w_ret_out[l], w_attn_out[l], w_out[l])
    return x


D_MIX = D_MODEL
N_Q_HEADS = 8
N_KV_HEADS = 2
GQA_GROUP = N_Q_HEADS // N_KV_HEADS
D_ATTN = N_Q_HEADS * HEAD_DIM
D_KV = N_KV_HEADS * HEAD_DIM
WINDOW = 128
ATT_BLOCK = 128
N_BUCKETS = 32
MAX_DISTANCE = 128
D_CONV = D_MIX // 4
CONV_WIDTH_2 = 3
D_SGU = D_MIX // 4
SGU_GROUPS = 4
SGU_GROUP_DIM = D_SGU // SGU_GROUPS
SGU_CHUNK = 128
IN_SPLITS_2 = (D_ATTN, D_KV, D_KV, D_CONV, D_CONV, D_CONV, D_SGU, D_SGU)
D_IN = D_ATTN + 2 * D_KV + 3 * D_CONV + 2 * D_SGU
PEER_HEADS = 8
PEER_TOPK = 16
N_KEYS = 128
N_EXPERTS = N_KEYS * N_KEYS
PEER_QDIM = 256
PEER_HALF = PEER_QDIM // 2
PEER_TOKEN_BLOCK = 128
NEG_INF = -1e30


def rms_norm_2(x, g):
    xf = x.astype(jnp.float32)
    y = xf * lax.rsqrt(jnp.mean(xf * xf, axis=-1, keepdims=True) + EPS)
    return (y * g.astype(jnp.float32)).astype(x.dtype)

def t5_causal_bucket(dist):
    max_exact = N_BUCKETS // 2
    d = jnp.maximum(dist, 0)
    log_ratio = jnp.log(jnp.maximum(d, 1).astype(jnp.float32) / max_exact) / math.log(MAX_DISTANCE / max_exact)
    large = max_exact + (log_ratio * (N_BUCKETS - max_exact)).astype(jnp.int32)
    large = jnp.minimum(large, N_BUCKETS - 1)
    return jnp.where(d < max_exact, d, large)

def sliding_window_attention(q, k, v, sink, rel_bias):
    B, S = q.shape[0], q.shape[1]
    nb = S // ATT_BLOCK
    qb = q.reshape(B, nb, ATT_BLOCK, N_KV_HEADS, GQA_GROUP, HEAD_DIM)
    kb = k.reshape(B, nb, ATT_BLOCK, N_KV_HEADS, HEAD_DIM)
    vb = v.reshape(B, nb, ATT_BLOCK, N_KV_HEADS, HEAD_DIM)

    def with_prev(t):
        prev = jnp.pad(t[:, :-1], ((0, 0), (1, 0), (0, 0), (0, 0), (0, 0)))
        return jnp.concatenate([prev, t], axis=2)

    kw, vw = with_prev(kb), with_prev(vb)
    logits = jnp.einsum('bnqkgd,bnskd->bnkgqs', qb, kw,
                        preferred_element_type=jnp.float32) * (HEAD_DIM ** -0.5)
    q_idx = jnp.arange(ATT_BLOCK)[:, None]
    s_idx = jnp.arange(2 * ATT_BLOCK)[None, :]
    dist = q_idx + ATT_BLOCK - s_idx
    in_window = (dist >= 0) & (dist < WINDOW)
    blk = jnp.arange(nb)[:, None, None]
    key_exists = (blk * ATT_BLOCK + s_idx[None] - ATT_BLOCK) >= 0
    mask = in_window[None] & key_exists
    bias = rel_bias.astype(jnp.float32)[t5_causal_bucket(dist)]
    bias = bias.transpose(2, 0, 1).reshape(N_KV_HEADS, GQA_GROUP, ATT_BLOCK, 2 * ATT_BLOCK)
    logits = jnp.where(mask[None, :, None, None], logits + bias, NEG_INF)
    sink_l = sink.astype(jnp.float32).reshape(1, 1, N_KV_HEADS, GQA_GROUP, 1, 1)
    m = jnp.maximum(jnp.max(logits, axis=-1, keepdims=True), sink_l)
    p = jnp.exp(logits - m)
    p = p / (jnp.sum(p, axis=-1, keepdims=True) + jnp.exp(sink_l - m))
    out = jnp.einsum('bnkgqs,bnskd->bnqkgd', p.astype(v.dtype), vw)
    return out.reshape(B, S, D_ATTN)

def short_conv_mixer(b_gate, c_gate, h, conv_w):
    S = h.shape[1]
    z = c_gate * h
    zp = jnp.pad(z, ((0, 0), (CONV_WIDTH_2 - 1, 0), (0, 0)))
    conv = zp[:, 0:S] * conv_w[0]
    for j in range(1, CONV_WIDTH_2):
        conv = conv + zp[:, j:j + S] * conv_w[j]
    return b_gate * conv

def chunked_spatial_gating(u, v, w_s, b_s):
    B, S = u.shape[0], u.shape[1]
    nc = S // SGU_CHUNK
    vf = v.astype(jnp.float32).reshape(B, S, SGU_GROUPS, SGU_GROUP_DIM)
    mu = jnp.mean(vf, axis=-1, keepdims=True)
    var = jnp.mean(jnp.square(vf - mu), axis=-1, keepdims=True)
    vn = ((vf - mu) * lax.rsqrt(var + EPS)).astype(v.dtype)
    vn = vn.reshape(B, nc, SGU_CHUNK, SGU_GROUPS, SGU_GROUP_DIM)
    causal = jnp.tril(jnp.ones((SGU_CHUNK, SGU_CHUNK), dtype=w_s.dtype))
    w = w_s * causal[None]
    mixed = jnp.einsum('gts,bnsgc->bntgc', w, vn) + b_s.T[None, None, :, :, None]
    return u * mixed.reshape(B, S, D_SGU)

def peer_ffn(h, w_pq, sub_keys, expert_down, expert_up):
    B, S, D = h.shape
    tokens = h.reshape(-1, PEER_TOKEN_BLOCK, D)

    def block(t):
        T = t.shape[0]
        q = (t @ w_pq).reshape(T, PEER_HEADS, 2, PEER_HALF)
        s = jnp.einsum('thpk,hpnk->thpn', q, sub_keys, preferred_element_type=jnp.float32)
        top_s, top_i = lax.top_k(s, PEER_TOPK)
        cand_s = top_s[:, :, 0, :, None] + top_s[:, :, 1, None, :]
        cand_i = top_i[:, :, 0, :, None] * N_KEYS + top_i[:, :, 1, None, :]
        best_s, best_pos = lax.top_k(cand_s.reshape(T, PEER_HEADS, PEER_TOPK * PEER_TOPK), PEER_TOPK)
        experts = jnp.take_along_axis(cand_i.reshape(T, PEER_HEADS, PEER_TOPK * PEER_TOPK), best_pos, axis=-1)
        gate = jax.nn.softmax(best_s, axis=-1)
        u = expert_down[experts]
        act = jax.nn.gelu(jnp.einsum('td,thkd->thk', t, u, preferred_element_type=jnp.float32),
                          approximate=False)
        wgt = (gate * act).astype(t.dtype)
        vv = expert_up[experts]
        return jnp.einsum('thk,thkd->td', wgt, vv)

    return lax.map(block, tokens).reshape(B, S, D)

def hybrid_layer_2(x, c_act, rel_bias, w_ada, b_ada, norm1_g, norm2_g, w_in, q_norm_g, k_norm_g,
                 attn_sink, conv_w, sgu_w, sgu_b, out_norm_g, w_out, peer_wq, peer_sub_keys,
                 peer_down, peer_up):
    B, S = x.shape[0], x.shape[1]
    mod = (c_act @ w_ada + b_ada)[:, None, :]
    sh1, sc1, g1, sh2, sc2, g2 = jnp.split(mod, 6, axis=-1)
    h = rms_norm_2(x, norm1_g) * (1 + sc1) + sh1
    proj = h @ w_in
    split_pts = [int(i) for i in np.cumsum(IN_SPLITS_2)[:-1]]
    q, k, v, cb, cc, ch, su, sv = jnp.split(proj, split_pts, axis=-1)
    q = rms_norm_2(q.reshape(B, S, N_Q_HEADS, HEAD_DIM), q_norm_g)
    k = rms_norm_2(k.reshape(B, S, N_KV_HEADS, HEAD_DIM), k_norm_g)
    v = v.reshape(B, S, N_KV_HEADS, HEAD_DIM)
    y_attn = sliding_window_attention(q, k, v, attn_sink, rel_bias)
    y_conv = short_conv_mixer(cb, cc, ch, conv_w)
    y_sgu = chunked_spatial_gating(su, sv, sgu_w, sgu_b)
    ga, gc, gs = jnp.split(out_norm_g, [D_ATTN, D_ATTN + D_CONV])
    merged = jnp.concatenate([rms_norm_2(y_attn, ga), rms_norm_2(y_conv, gc), rms_norm_2(y_sgu, gs)], axis=-1)
    x = x + g1 * (merged @ w_out)
    h2 = rms_norm_2(x, norm2_g) * (1 + sc2) + sh2
    x = x + g2 * peer_ffn(h2, peer_wq, peer_sub_keys, peer_down, peer_up)
    return x

def second_inputs(seed: int = 0) -> dict:
    key = jax.random.key(seed)
    ks = jax.random.split(key, 20)
    f32 = jnp.float32
    nrm = lambda k, shape, s: jax.random.normal(k, shape, f32) * s
    return {
        "x": nrm(ks[0], (BATCH, SEQ, D_MODEL), 1.0),
        "c": nrm(ks[1], (BATCH, D_MODEL), 1.0),
        "rel_bias": nrm(ks[2], (N_BUCKETS, N_Q_HEADS), 0.5),
        "w_ada": nrm(ks[3], (DEPTH, D_MODEL, 6 * D_MODEL), 0.5 * D_MODEL ** -0.5),
        "b_ada": nrm(ks[4], (DEPTH, 6 * D_MODEL), 0.02),
        "norm1_g": 1.0 + nrm(ks[5], (DEPTH, D_MODEL), 0.02),
        "norm2_g": 1.0 + nrm(ks[6], (DEPTH, D_MODEL), 0.02),
        "w_in": nrm(ks[7], (DEPTH, D_MODEL, D_IN), D_MODEL ** -0.5),
        "q_norm_g": 1.0 + nrm(ks[8], (DEPTH, HEAD_DIM), 0.02),
        "k_norm_g": 1.0 + nrm(ks[9], (DEPTH, HEAD_DIM), 0.02),
        "attn_sink": nrm(ks[10], (DEPTH, N_Q_HEADS), 0.5),
        "conv_w": nrm(ks[11], (DEPTH, CONV_WIDTH_2, D_CONV), CONV_WIDTH_2 ** -0.5),
        "sgu_w": nrm(ks[12], (DEPTH, SGU_GROUPS, SGU_CHUNK, SGU_CHUNK), SGU_CHUNK ** -0.5),
        "sgu_b": 1.0 + nrm(ks[13], (DEPTH, SGU_GROUPS, SGU_CHUNK), 0.02),
        "out_norm_g": 1.0 + nrm(ks[14], (DEPTH, D_MIX), 0.02),
        "w_out": nrm(ks[15], (DEPTH, D_MIX, D_MODEL), D_MIX ** -0.5),
        "peer_wq": nrm(ks[16], (DEPTH, D_MODEL, PEER_HEADS * PEER_QDIM), D_MODEL ** -0.5),
        "peer_sub_keys": nrm(ks[17], (DEPTH, PEER_HEADS, 2, N_KEYS, PEER_HALF), PEER_HALF ** -0.5),
        "peer_down": nrm(ks[18], (DEPTH, N_EXPERTS, D_MODEL), D_MODEL ** -0.5),
        "peer_up": nrm(ks[19], (DEPTH, N_EXPERTS, D_MODEL), 0.5 * PEER_HEADS ** -0.5),
    }

def second_block(x, c, rel_bias, w_ada, b_ada, norm1_g, norm2_g, w_in, q_norm_g, k_norm_g, attn_sink,
              conv_w, sgu_w, sgu_b, out_norm_g, w_out, peer_wq, peer_sub_keys, peer_down, peer_up):
    c_act = jax.nn.silu(c)
    for l in range(DEPTH):
        x = hybrid_layer_2(x, c_act, rel_bias, w_ada[l], b_ada[l], norm1_g[l], norm2_g[l], w_in[l],
                         q_norm_g[l], k_norm_g[l], attn_sink[l], conv_w[l], sgu_w[l], sgu_b[l],
                         out_norm_g[l], w_out[l], peer_wq[l], peer_sub_keys[l], peer_down[l], peer_up[l])
    return x


def setup_inputs(seed=0):
    out = dict(first_inputs(seed))
    for name, value in second_inputs(seed + 1).items():
        if name != "x":
            out[name + "_2"] = value
    return out


def reference(
    x, norm_g, w_in, b_gate, conv_dw, conv_b, conv_ln_g, conv_ln_b, ret_decay, q_norm_g,
    k_norm_g, attn_sink, w_conv_out, w_ret_out, w_attn_out, w_out, c_2, rel_bias_2, w_ada_2,
    b_ada_2, norm1_g_2, norm2_g_2, w_in_2, q_norm_g_2, k_norm_g_2, attn_sink_2, conv_w_2,
    sgu_w_2, sgu_b_2, out_norm_g_2, w_out_2, peer_wq_2, peer_sub_keys_2, peer_down_2, peer_up_2,
):
    x = first_block(
        x, norm_g, w_in, b_gate, conv_dw, conv_b, conv_ln_g, conv_ln_b, ret_decay, q_norm_g,
        k_norm_g, attn_sink, w_conv_out, w_ret_out, w_attn_out, w_out,
    )
    return second_block(
        x, c_2, rel_bias_2, w_ada_2, b_ada_2, norm1_g_2, norm2_g_2, w_in_2, q_norm_g_2,
        k_norm_g_2, attn_sink_2, conv_w_2, sgu_w_2, sgu_b_2, out_norm_g_2, w_out_2, peer_wq_2,
        peer_sub_keys_2, peer_down_2, peer_up_2,
    )


_drawn_inputs = setup_inputs


def setup_inputs(seed=0):
    import zlib

    import numpy as np

    out = dict(_drawn_inputs(seed))
    spreads = {}
    factors = {'conv_b': 4.766,
     'conv_ln_g': 7.603,
     'conv_ln_b': 8.0,
     'q_norm_g': 8.0,
     'k_norm_g': 8.0,
     'attn_sink': 8.0,
     'norm1_g_2': 6.029,
     'norm2_g_2': 8.0,
     'q_norm_g_2': 8.0,
     'k_norm_g_2': 8.0,
     'attn_sink_2': 22.073,
     'sgu_b_2': 8.0,
     'out_norm_g_2': 6.944}
    for name, (base, spread) in spreads.items():
        noise = np.random.default_rng([zlib.crc32(name.encode()), seed]).standard_normal(out[name].shape)
        drawn = base * np.exp(spread * noise) if base else spread * noise
        out[name] = __import__('jax').numpy.asarray(drawn.astype(out[name].dtype))
    for name, factor in factors.items():
        out[name] = (out[name] * factor).astype(out[name].dtype)
    return out
```

```python
import numpy as np
from contextlib import ExitStack

import concourse.bass as bass
from concourse import mybir

F32 = mybir.dt.float32
F32R = mybir.dt.float32r
U32 = mybir.dt.uint32
ACT = mybir.ActivationFunctionType
ALU = mybir.AluOpType
AX = mybir.AxisListType

P = 128
DEPTH = 2
D = 1024
KT = D // P
T = 256
NT = T // P
EPS = 1e-6
TAPS = 31
PADC = TAPS // 2
UNIT = 2048
CH = 512
NEG = -1e30

GLU_A, GLU_B, CGATE, RQ, RK, RV, RG, AQ, AK, AV, AG, GL = (
    0, 1024, 2048, 3072, 4096, 5120, 7168, 9216, 10240, 10496, 10752, 11776)


class Plan:

    def __init__(self):
        self.steps, self.units, self.slots = [], 0, 0

    def add(self, name, kind, j=0, units=0, slots=0):
        self.steps.append(dict(name=name, kind=kind, j=j, u=self.units, nu=units, n=self.slots, ns=slots))
        self.units += units
        self.slots += slots


def plan_first():
    pl, src = Plan(), []

    def half_units(w, c0, rows=(0,)):
        for r0 in rows:
            for h in (0, 1):
                src.append((w, r0 + h * 512, c0, "A"))

    def wide_unit(w, c0):
        src.append((w, 0, c0, "B"))

    for j in range(4):
        wide_unit("w_in", GLU_B + 256 * j)
        pl.add("glu_b", "B", j, 1, 1)
        wide_unit("w_in", GLU_A + 256 * j)
        pl.add("glu_a", "B", j, 1, 1)
    for j in range(4):
        wide_unit("w_in", CGATE + 256 * j)
        pl.add("cgate", "B", j, 1, 1)
    half_units("w_in", AQ)
    pl.add("aq", "A", 0, 2, 2)
    half_units("w_in", AQ + CH)
    pl.add("aq", "A", 1, 2, 2)
    pl.add("tq", "T", 0)
    half_units("w_in", AK)
    pl.add("akv", "A", 0, 2, 2)
    pl.add("tq", "T", 1)
    half_units("w_in", AG)
    pl.add("agate", "A", 0, 2, 2)
    pl.add("tk", "T", 0)
    half_units("w_in", AG + CH)
    pl.add("agate", "A", 1, 2, 2)
    for h in range(4):
        wide_unit("w_in", RQ + 256 * h)
        pl.add("rq", "B", h, 1, 1)
        wide_unit("w_in", RK + 256 * h)
        pl.add("rk", "B", h, 1, 1)
    for c in range(2):
        half_units("w_in", GL + CH * c)
        pl.add("g0", "A", c, 2, 2)
    pl.add("conv_norm", "T")
    for c in range(2):
        half_units("w_conv_out", CH * c)
        pl.add("out0", "A", c, 2, 2)
    for c in range(4):
        half_units("w_in", RV + CH * c)
        pl.add("rv", "A", c, 2, 2)
    pl.add("attention", "T", slots=8)
    for c in range(2):
        half_units("w_in", GL + 2048 + CH * c)
        pl.add("g2", "A", c, 2, 2)
    pl.add("attn_act", "T")
    for c in range(2):
        half_units("w_attn_out", CH * c)
        pl.add("out2", "A", c, 2, 2)
    for c in range(4):
        half_units("w_in", RG + CH * c)
        pl.add("rgate", "A", c, 2, 2)
    for c in range(2):
        half_units("w_in", GL + 1024 + CH * c)
        pl.add("g1", "A", c, 2, 2)
    pl.add("retention", "T", slots=8)
    for c in range(2):
        half_units("w_ret_out", CH * c, (0, 1024))
        pl.add("out1", "A", c, 4, 2)
    pl.add("merge_act", "T")
    for c in range(2):
        half_units("w_out", CH * c)
        pl.add("final", "A", c, 2, 2)
    assert len(src) == pl.units
    return pl, src


PLAN1, SRC1 = plan_first()
U1 = PLAN1.units


class Steps:

    def __init__(self, engine, sem):
        self.engine, self.sem, self.n = engine, sem, 0

    def step(self, ins):
        ins.then_inc(self.sem, 1)
        self.n += 1
        return self.n

    def wait(self, n=None):
        self.engine.wait_ge(self.sem, self.n if n is None else n)

    def link(self, ins):
        self.step(ins)
        self.wait()


def arena(nc, base):
    at = [base]

    def place(name, shape, dtype=F32, offset=None):
        size = 4
        for s in shape[1:]:
            size *= s
        if offset is None:
            offset = at[0]
            at[0] += (size + 31) // 32 * 32
        return nc.alloc_sbuf_tensor_at(name, shape, dtype, offset=offset)

    place.at = at
    return place


def fp32_pieces(w_hi, w_lo, x_hi, x_lo):
    return ((w_hi, x_hi), (w_hi, x_lo), (w_lo, x_hi))


CONSTS = dict(ident=128, cosr=256, sinr=256, mask=512, pos=512, neg=512, cosa=16, sina=16, iota=128, caus=128)


def const_offsets():
    at, out = 0, {}
    for k, n in CONSTS.items():
        out[k] = (at, n)
        at += n
    return out, at


COFF, CN = const_offsets()
P1 = dict(norm_g=8, dw=8 * TAPS, db=8, ln_g=8, ln_b=8, qg=64, kg=64, sink=16, decay=8)


def offsets(table):
    at, out = 0, {}
    for k, n in table.items():
        out[k] = (at, n)
        at += n
    return out, at


P1OFF, P1N = offsets(P1)


def first_layer(nc, env, l, inp):
    x_dram = env["xd"]
    pb = arena(nc, env["base1"])
    Xr = pb("f_x", [P, NT, D])
    n1 = COFF["iota"][0]
    CO = pb("f_const", [P, n1])
    PA = pb("f_par", [P, P1N])
    BG = pb("f_bgate", [P, D])
    con = {k: CO[:, a:a + n] for k, (a, n) in COFF.items() if a < n1}
    par = {k: PA[:, a:a + n] for k, (a, n) in P1OFF.items()}
    h_hi, h_lo = env["h_hi"], env["h_lo"]
    NRAW, NW = 2, 3
    raw = pb("f_raw", [P, NRAW, UNIT])
    w_hi = pb("f_whi", [P, NW, UNIT], F32R)
    w_lo = pb("f_wlo", [P, NW, UNIT], F32R)
    a_hi = pb("f_ahi", [P, KT, T], F32R)
    a_lo = pb("f_alo", [P, KT, T], F32R)
    ones = pb("f_ones", [P, P], offset=pb.at[0])
    merged = pb("f_merged", [P, NT, D])
    tg = pb("f_tg", [P, NT, D])
    tmp = pb("f_tmp", [P, 4, CH])
    stat = pb("f_stat", [P, 288])
    minus_half = pb("f_mhalf", [P, 8])
    rt = pb("f_rt", [P, 2, P])
    conv_at = pb.at[0]
    VW = T + 2 * PADC
    vpad = pb("f_vpad", [P, KT, VW])
    cy = pb("f_cy", [P, KT, T])
    cg = pb("f_cg", [P, KT, T])
    rv = pb("f_rv", [P, NT, 2048], offset=conv_at)
    pt = pb("f_pt", [P, 2, CH], offset=conv_at + 16384)
    attn_at = pb.at[0]
    qT = pb("f_qT", [P, KT, T])
    kT = pb("f_kT", [P, 4, T])
    av = pb("f_av", [P, NT, T])
    ag = pb("f_ag", [P, NT, D])
    rg = pb("f_rg", [P, NT, 2048], offset=attn_at)
    rqT = pb("f_rqT", [P, KT, T])
    rkT = pb("f_rkT", [P, KT, T])
    assert pb.at[0] <= nc.sbuf_usable_end, (pb.at[0], nc.sbuf_usable_end)
    dec = pb("f_dec", [P, 2, CH], offset=conv_at + 16384)
    sd = tmp
    rog = pb("f_rog", [P, NT, CH], offset=conv_at + 20480)
    tmpx = tmp[:, :, :].rearrange("p (t a) n -> p t (a n)", t=NT)
    rtw = rt[:, :, :].rearrange("p a n -> p (a n)")
    tmpx8 = tmp[:, :, :].rearrange("p a (b n) -> p (a b) n", b=2)
    sm = tmp[:, :, :].rearrange("p (t a) n -> p t (a n)", t=2)
    qn = rqT[:, :, :].rearrange("p (t j b) n -> p t j (b n)", t=NT, j=2)
    kd = rkT[:, 0:4, :].rearrange("p (t b) n -> p t (b n)", t=NT)
    SS, RS, ASS, ARS, NMX, SUM, ES, RDEN, MV, RRS, BST, NSINK = (
        stat[:, a:b] for a, b in ((0, 2), (2, 4), (8, 56), (56, 104), (104, 136), (136, 168), (168, 200), (168, 200),
                                  (200, 216), (216, 224), (224, 272), (272, 288)))

    with ExitStack() as cx:
        psA = cx.enter_context(nc.psum_tensor("f_psA", [P, 4, CH], F32))
        psS = cx.enter_context(nc.psum_tensor("f_psS", [P, 4, CH], F32))
        names = """in_x in_par in_bg raw0 raw1 hi_ready lo_ready unit_done acc_read small_ready small_read
            dve_step pool_step const_ready par_ready x_sq x_rstd x_norm h_hi_ready tanh_ready g_t
            a_sq a_ss a_rstd a_qn act_hi act_lo conv_y conv_sq conv_sd conv_u conv_t conv_p
            s_ready s_masked s_negmax s_exp s_sink pt_ready pt_read o_ready m_add
            decay_exp dec_arg dec_ready ro_ready r_var r_rstd r_og m_done x_done out_x""".split()
        S = {n: cx.enter_context(nc.semaphore("f_" + n)) for n in names}
        raw_in = [S["raw0"], S["raw1"]]
        steps = PLAN1.steps
        unit_step = {}
        for s in steps:
            for u in range(s["u"], s["u"] + s["nu"]):
                unit_step[u] = s
        by = {(s["name"], s["j"]): s for s in steps}

        small, m = {}, 0
        for name, count in (("norm", 4), ("tq0", 2), ("tq1", 2), ("tk", 2), ("conv_norm", 2)):
            small[name] = m
            m += count
        m_attention = m
        small_after = {}
        for name, count in (("attn_act", 4), ("ret", 12), ("merge_act", 4)):
            small_after[name] = m
            m += count
        small.update(small_after)

        def done(name, j=0):
            s = by[(name, j)]
            return s["u"] + s["nu"]

        def bias_of(branch):
            return inp["bgate"][bass.ds(l * 3 + branch, 1), :, :].rearrange("o p n -> p (o n)")

        with nc.Block() as block:

            @block.sync
            def _(sp):
                sp.dma_start(Xr[:, :, :], x_dram).then_inc(S["in_x"], 16)
                sp.dma_start(CO[:, :], inp["consts"][:, 0:n1]).then_inc(S["in_par"], 16)
                sp.dma_start(PA[:, :], inp["par1"][bass.ds(l, 1), :, :].rearrange("o p n -> p (o n)")).then_inc(S["in_par"], 16)

                def load(u, k):
                    src = inp["ws1"][bass.ds(l * U1 + u, 1), :, :].rearrange("o p n -> p (o n)")
                    sp.dma_start(raw[:, k, :], src).then_inc(raw_in[k], 16)

                sp.dma_start(BG[:, :], bias_of(0)).then_inc(S["in_bg"], 16)
                for k in range(NRAW):
                    load(k, k)
                with sp.Fori(1, U1 // NRAW) as i:
                    for k in range(NRAW):
                        sp.wait_ge(S["lo_ready"], i * NRAW + (k + 1 - NRAW))
                        load(i * NRAW + k, k)
                sp.wait_ge(S["x_done"], 4)
                sp.dma_start(x_dram, Xr[:, :, :]).then_inc(S["out_x"], 16)
                sp.wait_ge(S["out_x"], 16)

            @block.tensor
            def _(pe):
                ident = con["ident"]
                pe.wait_ge(S["in_par"], 32)

                def small_bank(i):
                    if i >= 4:
                        pe.wait_ge(S["small_read"], i - 3)
                    return psS[:, i % 4, :]

                def transposes(first, src, waits=None):
                    for b in range(4):
                        bank = small_bank(first + b)
                        if waits:
                            waits(b)
                        for kk in range(2):
                            for t in range(NT):
                                c = 2 * b + kk
                                last = nc.tensor.transpose(bank[:, kk * T + t * P:kk * T + (t + 1) * P],
                                                           src[:, t, c * P:(c + 1) * P], ident)
                        last.then_inc(S["small_ready"], 1)

                pe.wait_ge(S["x_norm"], 2)
                transposes(small["norm"], tmpx)
                pe.wait_ge(S["small_read"], small["norm"] + 4)
                for s in steps:
                    name, kind, j, n = s["name"], s["kind"], s["j"], s["n"]
                    if s["ns"] and n + s["ns"] > 4 and kind != "T":
                        pe.wait_ge(S["acc_read"], n + s["ns"] - 4)
                    if kind == "B":
                        u = s["u"]
                        pe.wait_ge(S["lo_ready"], u + 1)
                        wh, wl = w_hi[:, u % NW, :], w_lo[:, u % NW, :]
                        for f in range(2):
                            for kt in range(KT):
                                c = kt * 256 + f * P
                                for i, (w, x) in enumerate(fp32_pieces(wh, wl, h_hi, h_lo)):
                                    last = nc.tensor.matmul(psA[:, n % 4, f * T:(f + 1) * T], w[:, c:c + P], x[:, kt, :],
                                                            start=kt == 0 and i == 0, stop=kt == KT - 1 and i == 2)
                        last.then_inc(S["unit_done"], 1)
                    elif kind == "A":
                        if name == "out0":
                            pe.wait_ge(S["act_lo"], 1)
                        elif name == "out2":
                            pe.wait_ge(S["small_read"], small["attn_act"] + 4)
                        elif name == "out1":
                            pe.wait_ge(S["small_read"], small["ret"] + 12)
                        elif name == "final":
                            pe.wait_ge(S["small_read"], small["merge_act"] + 4)
                        own = name in ("out0", "out2", "final")
                        for v in range(s["nu"]):
                            u = s["u"] + v
                            pe.wait_ge(S["lo_ready"], u + 1)
                            wh, wl = w_hi[:, u % NW, :], w_lo[:, u % NW, :]
                            xh, xl = (a_hi, a_lo) if own or (name == "out1" and v < 2) else (h_hi, h_lo)
                            for t in range(NT):
                                for k in range(4):
                                    kt = (4 * v + k) % KT
                                    ts_ = slice(t * P, (t + 1) * P)
                                    for i, (x, w) in enumerate(fp32_pieces(xh, xl, wh, wl)):
                                        last = nc.tensor.matmul(psA[:, (n + t) % 4, :], x[:, kt, ts_],
                                                                w[:, k * CH:(k + 1) * CH],
                                                                start=v == 0 and k == 0 and i == 0,
                                                                stop=v == s["nu"] - 1 and k == 3 and i == 2)
                            last.then_inc(S["unit_done"], 1)
                    elif name == "tq":
                        for b in range(2):
                            bank = small_bank(small[f"tq{j}"] + b)
                            pe.wait_ge(S["a_qn"], NT * (j + 1))
                            for kk in range(2):
                                for t in range(NT):
                                    c = 2 * b + kk
                                    last = nc.tensor.transpose(bank[:, kk * T + t * P:kk * T + (t + 1) * P],
                                                               qn[:, t, j, c * P:(c + 1) * P], ident)
                            last.then_inc(S["small_ready"], 1)
                    elif name == "tk":
                        for b in range(2):
                            bank = small_bank(small["tk"] + b)
                            pe.wait_ge(S["a_qn"], NT * 3)
                            for kk in range(2):
                                for t in range(NT):
                                    c = 2 * b + kk
                                    last = nc.tensor.transpose(bank[:, kk * T + t * P:kk * T + (t + 1) * P],
                                                               kd[:, t, c * P:(c + 1) * P], ident)
                            last.then_inc(S["small_ready"], 1)
                    elif name == "conv_norm":
                        for i, (ready, src) in enumerate((("conv_y", cy), ("conv_sq", tmpx8))):
                            bank = small_bank(small["conv_norm"] + i)
                            pe.wait_ge(S[ready], 1)
                            for kt in range(KT):
                                last = nc.tensor.matmul(bank[:, 0:T], ones[:, :], src[:, kt, :], start=kt == 0, stop=kt == KT - 1)
                            last.then_inc(S["small_ready"], 1)
                    elif name == "attention":
                        pe.wait_ge(S["small_read"], m_attention)

                        def scores(p):
                            if p:
                                pe.wait_ge(S["s_masked"], p)
                            for hh in range(2):
                                r = slice(64 * hh, 64 * hh + 64)
                                for t in range(NT):
                                    last = nc.tensor.matmul(psS[:, hh, t * T:(t + 1) * T], qT[r, p, t * P:(t + 1) * P],
                                                            kT[r, p // 2, :], start=True, stop=True)
                            last.then_inc(S["s_ready"], 1)

                        scores(0)
                        for p in range(8):
                            if p < 7:
                                scores(p + 1)
                            pe.wait_ge(S["s_exp"], p + 1)
                            if p:
                                pe.wait_ge(S["pt_read"], 2 * p)
                            for hh in range(2):
                                for t in range(NT):
                                    for jt in range(2):
                                        c = (t * 2 + jt) * P
                                        last = nc.tensor.transpose(psS[:, 2 + hh, c:c + P],
                                                                   sm[:, p % 2, (hh * 2 + t) * T + jt * P:(hh * 2 + t) * T + (jt + 1) * P], ident)
                            last.then_inc(S["pt_ready"], 1)
                            nn = n + p
                            pe.wait_ge(S["acc_read"], nn - 3)
                            pe.wait_ge(S["pt_read"], 2 * p + 2)
                            for hh in range(2):
                                for t in range(NT):
                                    c = (hh * 2 + t) * 64
                                    for jt in range(2):
                                        last = nc.tensor.matmul(psA[:, nn % 4, c:c + 64], pt[:, hh, (t * 2 + jt) * P:(t * 2 + jt + 1) * P],
                                                                av[:, jt, (p // 2) * 64:(p // 2) * 64 + 64],
                                                                start=jt == 0, stop=jt == 1)
                            last.then_inc(S["o_ready"], 1)
                        pe.wait_ge(S["s_masked"], 8)
                    elif name == "attn_act":
                        pe.wait_ge(S["acc_read"], by[("attention", 0)]["n"] + 8)
                        transposes(small["attn_act"], ag)
                    elif name == "merge_act":
                        pe.wait_ge(S["m_done"], 4)
                        transposes(small["merge_act"], merged)
                    elif name == "retention":
                        m0 = small["ret"]

                        def rscores(h):
                            bank = small_bank(m0 + 3 * h)
                            for jt in range(2):
                                for k in range(2):
                                    last = nc.tensor.matmul(bank[:, jt * T:(jt + 1) * T], rkT[:, 2 * h + k, jt * P:(jt + 1) * P],
                                                            rqT[:, 2 * h + k, :], start=k == 0, stop=k == 1)
                            last.then_inc(S["small_ready"], 1)

                        rscores(0)
                        for h in range(4):
                            nn = n + 2 * h
                            pe.wait_ge(S["acc_read"], nn - 2)
                            pe.wait_ge(S["small_read"], m0 + 3 * h + 1)
                            for t in range(NT):
                                for jt in range(2):
                                    last = nc.tensor.matmul(psA[:, (nn + t) % 4, :], sd[:, h % 2, jt * T + t * P:jt * T + (t + 1) * P],
                                                            rv[:, jt, h * CH:(h + 1) * CH], start=jt == 0, stop=jt == 1)
                            last.then_inc(S["ro_ready"], 1)
                            for b in range(2):
                                bank = small_bank(m0 + 3 * h + 1 + b)
                                pe.wait_ge(S["r_og"], 2 * h + 2)
                                for kk in range(2):
                                    for t in range(NT):
                                        c = 2 * b + kk
                                        last = nc.tensor.transpose(bank[:, kk * T + t * P:kk * T + (t + 1) * P],
                                                                   rog[:, t, c * P:(c + 1) * P], ident)
                                last.then_inc(S["small_ready"], 1)
                            if h < 3:
                                rscores(h + 1)

            tanh_of = []
            for s in steps:
                if s["name"] in ("glu_b", "cgate"):
                    tanh_of.append((s["name"], s["n"], s["n"] + 1 if s["name"] == "cgate" else s["n"] + 2))
                elif s["name"] in ("agate", "rgate"):
                    tanh_of += [(s["name"], s["n"] + t, s["n"] + t + 1) for t in range(NT)]
            tanh_at = {n: q for q, (_, n, _) in enumerate(tanh_of)}

            @block.scalar
            def _(act):
                converted = [0]

                def heads(upto):
                    while converted[0] <= min(upto, U1 - 1):
                        u = converted[0]
                        act.wait_ge(raw_in[u % NRAW], 16 * (u // NRAW + 1))
                        if u >= NW:
                            act.wait_ge(S["unit_done"], u - NW + 1)
                        nc.scalar.activation(w_hi[:, u % NW, :], raw[:, u % NRAW, :], ACT.Copy).then_inc(S["hi_ready"], 1)
                        converted[0] += 1

                def half_tanh(n):
                    q = tanh_at[n]
                    if q >= 4:
                        act.wait_ge(S["acc_read"], tanh_of[q - 4][2])
                    nc.scalar.activation(tmp[:, q % 4, :], psA[:, n % 4, :], ACT.Tanh, scale=0.5).then_inc(S["tanh_ready"], 1)

                def cast_heads(first, dst, banks):
                    for b in range(banks):
                        act.wait_ge(S["small_ready"], first + b + 1)
                        nc.scalar.activation(dst[:, 2 * b:2 * b + 2, :], psS[:, (first + b) % 4, :].rearrange("p (a n) -> p a n", a=2),
                                             ACT.Copy, scale=0.5).then_inc(S["act_hi"], 1)

                act.wait_ge(S["in_x"], 16)
                for t in range(NT):
                    nc.scalar.activation(tg[:, t, :], Xr[:, t, :], ACT.Square, accum_out=SS[:, t:t + 1]).then_inc(S["x_sq"], 1)
                act.wait_ge(S["in_par"], 32)
                nc.scalar.activation(par["decay"], par["decay"], ACT.Exp).then_inc(S["decay_exp"], 1)
                heads(2)
                for kt in range(KT):
                    act.wait_ge(S["small_ready"], small["norm"] + kt // 2 + 1)
                    nc.scalar.activation(h_hi[:, kt, :], psS[:, (small["norm"] + kt // 2) % 4, (kt % 2) * T:(kt % 2 + 1) * T],
                                         ACT.Copy, scale=par["norm_g"][:, kt:kt + 1]).then_inc(S["h_hi_ready"], 1)
                asq = 0
                for s in steps:
                    name, j, n = s["name"], s["j"], s["n"]
                    if s["nu"]:
                        heads(s["u"] + s["nu"] + 1)
                        if name in ("glu_b", "cgate", "agate", "rgate", "aq", "akv"):
                            act.wait_ge(S["unit_done"], s["u"] + s["nu"])
                    if name in ("glu_b", "cgate"):
                        half_tanh(n)
                    elif name in ("agate", "rgate"):
                        if name == "rgate" and j == 0:
                            act.wait_ge(S["m_add"], 4)
                        for t in range(NT):
                            half_tanh(n + t)
                    elif name in ("aq", "akv"):
                        w = CH if name == "aq" else 256
                        for t in range(NT):
                            if asq >= 4:
                                act.wait_ge(S["a_ss"], asq - 3)
                            nc.scalar.activation(tg[:, (asq % 4) // 2, (asq % 2) * CH:(asq % 2) * CH + w], psA[:, (n + t) % 4, 0:w],
                                                 ACT.Square).then_inc(S["a_sq"], 1)
                            asq += 1
                    elif name in ("g0", "g1", "g2"):
                        for t in range(NT):
                            act.wait_ge(S["acc_read"], n + t + 1)
                            g = tg[:, t, j * CH:(j + 1) * CH]
                            nc.scalar.activation(g, g, ACT.Tanh, scale=0.5).then_inc(S["g_t"], 1)
                        if j == 1 and name != "g1":
                            act.dma_start(BG[:, :], bias_of(2 if name == "g0" else 1)).then_inc(S["in_bg"], 16)
                    elif name == "conv_norm":
                        act.wait_ge(S["small_read"], small["conv_norm"] + 1)
                        nc.scalar.activation(tmpx8, cy[:, :, :], ACT.Square).then_inc(S["conv_sq"], 1)
                        act.wait_ge(S["small_read"], small["conv_norm"] + 2)
                        nc.scalar.activation(rtw, rtw, ACT.Sqrt).then_inc(S["conv_sd"], 1)
                        act.wait_ge(S["conv_u"], 1)
                        nc.scalar.activation(tmpx8, cy[:, :, :], ACT.Tanh, scale=0.5).then_inc(S["conv_t"], 1)
                        act.wait_ge(S["conv_p"], 1)
                        nc.scalar.activation(a_hi[:, :, :], cy[:, :, :], ACT.Copy, scale=0.25).then_inc(S["act_hi"], 1)
                    elif name == "attention":

                        def exps(p):
                            act.wait_ge(S["s_negmax"], p + 1)
                            for i in range(4):
                                row = sm[:, p % 2, i * T:(i + 1) * T]
                                c = 4 * p + i
                                ins = nc.scalar.activation(row, row, ACT.Exp, bias=NMX[:, c:c + 1], accum_out=SUM[:, c:c + 1])
                            ins.then_inc(S["s_exp"], 1)
                            for hh in range(2):
                                c = 4 * p + 2 * hh
                                ins = nc.scalar.activation(ES[:, c:c + 2], NMX[:, c:c + 2], ACT.Exp,
                                                           bias=par["sink"][:, 2 * p + hh:2 * p + hh + 1])
                            ins.then_inc(S["s_sink"], 1)

                        exps(0)
                        for p in range(8):
                            if p < 7:
                                exps(p + 1)
                            act.wait_ge(S["pt_ready"], p + 1)
                            if p:
                                act.wait_ge(S["o_ready"], p)
                            for hh in range(2):
                                nc.scalar.activation(pt[:, hh, :], psS[:, 2 + hh, :], ACT.Copy).then_inc(S["pt_read"], 1)
                    elif name == "attn_act":
                        cast_heads(small["attn_act"], a_hi, 4)
                    elif name == "merge_act":
                        cast_heads(small["merge_act"], a_hi, 4)
                    elif name == "retention":

                        def decay(h):
                            act.wait_ge(S["dec_arg"], h + 1)
                            nc.scalar.activation(dec[:, h % 2, :], dec[:, h % 2, :], ACT.Exp).then_inc(S["dec_ready"], 1)

                        decay(0)
                        decay(1)
                        for h in range(4):
                            dst = (a_hi if h < 2 else h_hi)[:, 4 * (h % 2):4 * (h % 2) + 4, :]
                            cast_heads(small["ret"] + 3 * h + 1, dst, 2)
                            if h < 2:
                                decay(h + 2)

            @block.gpsimd
            def _(pool):
                own = Steps(pool, S["pool_step"])

                def rstd(dst, src, width, scale, done):
                    own.link(nc.gpsimd.tensor_scalar(dst, src, scale, EPS, ALU.mult, ALU.add))
                    nc.gpsimd.tensor_tensor(dst, dst, minus_half[:, 0:width], ALU.pow).then_inc(done, 1)

                own.step(nc.gpsimd.memset(minus_half[:, :], -0.5))
                nc.gpsimd.memset(ones[:, :], 1.0 / D).then_inc(S["const_ready"], 1)
                nc.gpsimd.memset(vpad[:, :, 0:PADC], 0.0).then_inc(S["const_ready"], 1)
                nc.gpsimd.memset(vpad[:, :, PADC + T:VW], 0.0).then_inc(S["const_ready"], 1)
                own.wait()
                pool.wait_ge(S["x_sq"], NT)
                rstd(RS, SS, NT, 1.0 / D, S["x_rstd"])
                for i in range(6):
                    pool.wait_ge(S["a_ss"], i + 1)
                    w = 8 if i < 4 else 4
                    rstd(ARS[:, 8 * i:8 * i + w], ASS[:, 8 * i:8 * i + w], w, 1.0 / 64, S["a_rstd"])
                for h in range(4):
                    pool.wait_ge(S["r_var"], h + 1)
                    rstd(RRS[:, 2 * h:2 * h + 2], MV[:, 4 * h:4 * h + 4].rearrange("p (t k) -> p t k", k=2)[:, :, 1], 2, 1.0, S["r_rstd"])

            @block.vector
            def _(dve):
                own = Steps(dve, S["dve_step"])
                V = nc.vector
                converted = [0]

                def rests(upto):
                    while converted[0] <= min(upto, U1 - 1):
                        u = converted[0]
                        dve.wait_ge(S["hi_ready"], u + 1)
                        V.tensor_tensor(w_lo[:, u % NW, :], raw[:, u % NRAW, :], w_hi[:, u % NW, :].bitcast(F32),
                                        ALU.subtract).then_inc(S["lo_ready"], 1)
                        converted[0] += 1

                casts = [1]

                def cast_rests(first, dst_hi, dst_lo, banks):
                    for b in range(banks):
                        casts[0] += 1
                        dve.wait_ge(S["act_hi"], casts[0])
                        V.scalar_tensor_tensor(dst_lo[:, 2 * b:2 * b + 2, :].rearrange("p a n -> p (a n)"), psS[:, (first + b) % 4, :], 0.5,
                                               dst_hi[:, 2 * b:2 * b + 2, :].rearrange("p a n -> p (a n)").bitcast(F32),
                                               ALU.mult, ALU.subtract).then_inc(S["small_read"], 1)

                dve.wait_ge(S["in_par"], 32)
                own.step(V.tensor_scalar(par["dw"], par["dw"], 0.5, None, ALU.mult))
                own.step(V.tensor_scalar(par["qg"], par["qg"], 0.125, None, ALU.mult))
                own.step(V.tensor_scalar(NSINK, par["sink"], -1.0, None, ALU.mult))
                dve.wait_ge(S["decay_exp"], 1)
                own.step(V.tensor_scalar(par["decay"], par["decay"], -1.0, None, ALU.mult))
                dve.wait_ge(S["x_rstd"], 1)
                dve.wait_ge(S["in_x"], 16)
                for t in range(NT):
                    V.tensor_scalar(tmpx[:, t, :], Xr[:, t, :], RS[:, t:t + 1], None, ALU.mult).then_inc(S["x_norm"], 1)
                rests(2)
                for kt in range(KT):
                    dve.wait_ge(S["h_hi_ready"], kt - kt % 2 + 2)
                    ins = V.scalar_tensor_tensor(h_lo[:, kt, :], psS[:, (small["norm"] + kt // 2) % 4, (kt % 2) * T:(kt % 2 + 1) * T],
                                                 par["norm_g"][:, kt:kt + 1], h_hi[:, kt, :].bitcast(F32), ALU.mult, ALU.subtract)
                    ins.then_inc(S["small_read"], 1) if kt % 2 else own.step(ins)

                taps_total = KT * TAPS
                tap_done = {}
                tap_next = [0]

                def taps(upto):
                    for i in range(tap_next[0], min(upto, taps_total)):
                        pair, r = divmod(i, 2 * TAPS)
                        k, f = divmod(r, 2)
                        ft = 2 * pair + f
                        w = par["dw"][:, ft * TAPS + k:ft * TAPS + k + 1]
                        v = vpad[:, ft, k:k + T]
                        if k == 0:
                            if f == 0:
                                dve.wait_ge(S["const_ready"], 3)
                                dve.wait_ge(S["acc_read"], by[("glu_a", pair)]["n"] + 1)
                            ins = V.tensor_scalar(cy[:, ft, :], v, w, par["db"][:, ft:ft + 1], ALU.mult, ALU.add)
                        else:
                            own.wait(tap_done[i - 2])
                            ins = V.scalar_tensor_tensor(cy[:, ft, :], v, w, cy[:, ft, :], ALU.mult, ALU.add)
                        if i == taps_total - 1:
                            ins.then_inc(S["conv_y"], 1)
                        else:
                            tap_done[i] = own.step(ins)
                    tap_next[0] = max(tap_next[0], min(upto, taps_total))

                u_tap0, u_tap1 = by[("cgate", 0)]["u"], by[("conv_norm", 0)]["u"]
                bc8 = lambda ap: ap.rearrange("p (o n) -> p o n", o=1).to_broadcast([P, KT, T])

                def rotate_heads(x, t, heads_):
                    cos = con["cosa"][:, 8 * t:8 * t + 8].rearrange("p (a b n) -> p a b n", a=1, b=1).to_broadcast([P, heads_, 2, 8])
                    sin = con["sina"][:, 8 * t:8 * t + 8].rearrange("p (a b n) -> p a b n", a=1, b=1).to_broadcast([P, heads_, 2, 8])
                    xs = x[:, :, 0:16].rearrange("p h (b n) -> p h b n", b=2)
                    w = heads_ * 16
                    m1 = rt[:, 0, 0:w].rearrange("p (h b n) -> p h b n", h=heads_, b=2)
                    m2 = rt[:, 1, 0:w].rearrange("p (h b n) -> p h b n", h=heads_, b=2)
                    own.step(V.tensor_tensor(m1, xs, cos, ALU.mult))
                    own.link(V.tensor_tensor(m2, xs, sin, ALU.mult))
                    own.step(V.tensor_tensor(xs[:, :, 0, :], m1[:, :, 0, :], m2[:, :, 1, :], ALU.subtract))
                    return V.tensor_tensor(xs[:, :, 1, :], m1[:, :, 1, :], m2[:, :, 0, :], ALU.add)

                asq, aqn, gts, bgs = 0, 0, 0, 0
                for s in steps:
                    name, j, n = s["name"], s["j"], s["n"]
                    if s["nu"]:
                        rests(s["u"] + s["nu"] + 1)
                        dve.wait_ge(S["unit_done"], s["u"] + s["nu"])
                    A = [psA[:, (n + t) % 4, :] for t in range(NT)]
                    if name == "glu_a":
                        dve.wait_ge(S["tanh_ready"], tanh_at[n - 1] + 1)
                        for f in range(2):
                            V.scalar_tensor_tensor(vpad[:, 2 * j + f, PADC:PADC + T], tmp[:, tanh_at[n - 1] % 4, f * T:(f + 1) * T], 1.0,
                                                   A[0][:, f * T:(f + 1) * T], ALU.add, ALU.mult).then_inc(S["acc_read"], 1)
                    elif name == "cgate":
                        dve.wait_ge(S["tanh_ready"], tanh_at[n] + 1)
                        V.scalar_tensor_tensor(cg[:, 2 * j:2 * j + 2, :].rearrange("p a n -> p (a n)"), tmp[:, tanh_at[n] % 4, :], 1.0,
                                               A[0], ALU.add, ALU.mult).then_inc(S["acc_read"], 1)
                    elif name in ("agate", "rgate"):
                        dst = ag if name == "agate" else rg
                        for t in range(NT):
                            q = tanh_at[n + t]
                            dve.wait_ge(S["tanh_ready"], q + 1)
                            V.scalar_tensor_tensor(dst[:, t, j * CH:(j + 1) * CH], tmp[:, q % 4, :], 1.0, A[t],
                                                   ALU.add, ALU.mult).then_inc(S["acc_read"], 1)
                    elif name in ("aq", "akv"):
                        nh = 8 if name == "aq" else 4
                        for t in range(NT):
                            dve.wait_ge(S["a_sq"], asq + 1)
                            sq = tg[:, (asq % 4) // 2, (asq % 2) * CH:(asq % 2) * CH + nh * 64].rearrange("p (h n) -> p h n", n=64)
                            V.tensor_reduce(ASS[:, 8 * asq:8 * asq + nh], sq, AX.X, ALU.add).then_inc(S["a_ss"], 1)
                            asq += 1
                        for t in range(NT):
                            i = asq - NT + t
                            gain = (par["qg"] if nh == 8 else par["kg"]).rearrange("p (h n) -> p h n", h=1).to_broadcast([P, nh, 64])
                            if nh == 8:
                                x = qn[:, t, j, :].rearrange("p (h n) -> p h n", n=64)
                            else:
                                kx = kd[:, t, :].rearrange("p (h c n) -> p h c n", c=2, n=64)
                                x = kx[:, :, 0, :]
                                own.step(V.tensor_copy(av[:, t, :], A[t][:, 256:512]))
                            dve.wait_ge(S["a_rstd"], i + 1)
                            r = ARS[:, 8 * i:8 * i + nh].rearrange("p (h n) -> p h n", n=1).to_broadcast([P, nh, 64])
                            V.tensor_tensor(x, A[t][:, 0:nh * 64].rearrange("p (h n) -> p h n", n=64), r, ALU.mult).then_inc(S["acc_read"], 1)
                            dve.wait_ge(S["acc_read"], n + t + 1)
                            own.link(V.tensor_tensor(x, x, gain, ALU.mult))
                            ins = rotate_heads(x, t, nh)
                            if nh == 8:
                                ins.then_inc(S["a_qn"], 1)
                            else:
                                own.link(ins)
                                V.tensor_copy(kx[:, :, 1, :], x).then_inc(S["a_qn"], 1)
                    elif name in ("tq", "tk"):
                        m = small[f"tq{j}" if name == "tq" else "tk"]
                        dst = qT if name == "tq" else kT
                        for b in range(2):
                            dve.wait_ge(S["small_ready"], m + b + 1)
                            k = (4 * j if name == "tq" else 0) + 2 * b
                            V.tensor_copy(dst[:, k:k + 2, :].rearrange("p a n -> p (a n)"), psS[:, (m + b) % 4, :]).then_inc(S["small_read"], 1)
                    elif name in ("rq", "rk"):
                        dst = rqT if name == "rq" else rkT
                        cos = con["cosr"].rearrange("p (a n) -> p a n", a=1).to_broadcast([P, 2, T])
                        sin = con["sinr"].rearrange("p (a n) -> p a n", a=1).to_broadcast([P, 2, T])
                        x = A[0].rearrange("p (a n) -> p a n", a=2)
                        i = 0 if name == "rq" else 1
                        m1 = tg[:, i, 0:CH].rearrange("p (a n) -> p a n", a=2)
                        m2 = tg[:, i, CH:D].rearrange("p (a n) -> p a n", a=2)
                        own.step(V.tensor_tensor(m1, x, cos, ALU.mult))
                        V.tensor_tensor(m2, x, sin, ALU.mult).then_inc(S["acc_read"], 1)
                        dve.wait_ge(S["acc_read"], n + 1)
                        if (name, j) == ("rq", 0):
                            dve.wait_ge(S["small_ready"], small["tk"] + 2)
                        own.step(V.tensor_tensor(dst[:, 2 * j, :], m1[:, 0, :], m2[:, 1, :], ALU.subtract))
                        own.step(V.tensor_tensor(dst[:, 2 * j + 1, :], m1[:, 1, :], m2[:, 0, :], ALU.add))
                    elif name in ("g0", "g1", "g2"):
                        if j == 0:
                            bgs += 1
                            dve.wait_ge(S["in_bg"], 16 * bgs)
                            own.wait()
                        for t in range(NT):
                            V.tensor_tensor(tg[:, t, j * CH:(j + 1) * CH], A[t], BG[:, j * CH:(j + 1) * CH], ALU.add).then_inc(S["acc_read"], 1)
                    elif name in ("out0", "out1", "out2"):
                        for t in range(NT):
                            g = tg[:, t, j * CH:(j + 1) * CH]
                            m = merged[:, t, j * CH:(j + 1) * CH]
                            dve.wait_ge(S["g_t"], {"out0": 4, "out2": 8, "out1": 12}[name])
                            if name == "out0":
                                V.scalar_tensor_tensor(m, g, 1.0, A[t], ALU.add, ALU.mult).then_inc(S["acc_read"], 1)
                                continue
                            w = tmp[:, 2 + t, :]
                            V.scalar_tensor_tensor(w, g, 1.0, A[t], ALU.add, ALU.mult).then_inc(S["acc_read"], 1)
                            dve.wait_ge(S["acc_read"], n + t + 1)
                            V.tensor_tensor(m, m, w, ALU.add).then_inc(S["m_add" if name == "out2" else "m_done"], 1)
                    elif name == "conv_norm":
                        taps(taps_total)
                        dve.wait_ge(S["conv_y"], 1)
                        m = small["conv_norm"]
                        dve.wait_ge(S["small_ready"], m + 1)
                        V.tensor_tensor(cy[:, :, :], cy[:, :, :], bc8(psS[:, m % 4, 0:T]), ALU.subtract).then_inc(S["small_read"], 1)
                        dve.wait_ge(S["small_ready"], m + 2)
                        V.tensor_scalar(rtw, psS[:, (m + 1) % 4, 0:T], EPS, None, ALU.add).then_inc(S["small_read"], 1)
                        dve.wait_ge(S["conv_sd"], 1)
                        own.link(V.reciprocal(rtw, rtw))
                        own.link(V.tensor_tensor(cy[:, :, :], cy[:, :, :], bc8(rtw), ALU.mult))
                        for ft in range(KT):
                            ins = V.tensor_scalar(cy[:, ft, :], cy[:, ft, :], par["ln_g"][:, ft:ft + 1], par["ln_b"][:, ft:ft + 1], ALU.mult, ALU.add)
                            ins.then_inc(S["conv_u"], 1) if ft == KT - 1 else own.step(ins)
                        dve.wait_ge(S["conv_t"], 1)
                        flat = cy[:, :, :].rearrange("p a n -> p (a n)")
                        own.link(V.scalar_tensor_tensor(flat, tmpx8.rearrange("p a n -> p (a n)"), 1.0, flat, ALU.add, ALU.mult))
                        V.tensor_tensor(flat, flat, cg[:, :, :].rearrange("p a n -> p (a n)"), ALU.mult).then_inc(S["conv_p"], 1)
                        dve.wait_ge(S["act_hi"], 1)
                        V.scalar_tensor_tensor(a_lo[:, :, :].rearrange("p a n -> p (a n)"), flat, 0.25,
                                               a_hi[:, :, :].rearrange("p a n -> p (a n)").bitcast(F32), ALU.mult, ALU.subtract).then_inc(S["act_lo"], 1)
                    elif name == "rv":
                        for t in range(NT):
                            V.tensor_copy(rv[:, t, j * CH:(j + 1) * CH], A[t]).then_inc(S["acc_read"], 1)
                    elif name == "attention":

                        def masked(p):
                            dve.wait_ge(S["s_ready"], p + 1)
                            if p >= 2:
                                dve.wait_ge(S["pt_ready"], p - 1)
                            mask = con["mask"].rearrange("p (a n) -> p a n", a=1).to_broadcast([P, 2, CH])
                            V.tensor_tensor(sm[:, p % 2, :].rearrange("p (a n) -> p a n", a=2), psS[:, 0:2, :], mask, ALU.add).then_inc(S["s_masked"], 1)
                            dve.wait_ge(S["s_masked"], p + 1)
                            nm = NMX[:, 4 * p:4 * p + 4]
                            own.link(V.tensor_reduce(nm, sm[:, p % 2, :].rearrange("p (a n) -> p a n", n=T), AX.X, ALU.max, negate=True))
                            nm2 = nm.rearrange("p (h t) -> p h t", t=NT)
                            ns = NSINK[:, 2 * p:2 * p + 2].rearrange("p (h t) -> p h t", t=1).to_broadcast([P, 2, NT])
                            V.tensor_tensor(nm2, nm2, ns, ALU.min).then_inc(S["s_negmax"], 1)

                        masked(0)
                        for p in range(8):
                            if p < 7:
                                masked(p + 1)
                            c = slice(4 * p, 4 * p + 4)
                            dve.wait_ge(S["s_sink"], p + 1)
                            own.link(V.tensor_tensor(RDEN[:, c], SUM[:, c], ES[:, c], ALU.add))
                            own.link(V.reciprocal(RDEN[:, c], RDEN[:, c]))
                            dve.wait_ge(S["o_ready"], p + 1)
                            for i in range(4):
                                hh, t = divmod(i, 2)
                                g = ag[:, t, (2 * p + hh) * 64:(2 * p + hh + 1) * 64]
                                ins = V.scalar_tensor_tensor(g, psA[:, (n + p) % 4, i * 64:(i + 1) * 64], RDEN[:, 4 * p + i:4 * p + i + 1], g,
                                                             ALU.mult, ALU.mult)
                                ins.then_inc(S["acc_read"], 1) if i == 3 else own.step(ins)
                    elif name == "attn_act":
                        cast_rests(small["attn_act"], a_hi, a_lo, 4)
                    elif name == "merge_act":
                        cast_rests(small["merge_act"], a_hi, a_lo, 4)
                    elif name == "retention":

                        def decay_arg(h):
                            own.link(V.tensor_scalar(dec[:, h % 2, :], con["pos"], par["decay"][:, h:h + 1], None, ALU.mult))
                            V.scalar_tensor_tensor(dec[:, h % 2, :], con["neg"], par["decay"][:, 4 + h:5 + h], dec[:, h % 2, :],
                                                   ALU.mult, ALU.add).then_inc(S["dec_arg"], 1)

                        decay_arg(0)
                        decay_arg(1)
                        m0 = small["ret"]
                        for h in range(4):
                            dve.wait_ge(S["small_ready"], m0 + 3 * h + 1)
                            dve.wait_ge(S["dec_ready"], h + 1)
                            V.scalar_tensor_tensor(sd[:, h % 2, :], psS[:, (m0 + 3 * h) % 4, :], 1.0 / 16, dec[:, h % 2, :],
                                                   ALU.mult, ALU.mult).then_inc(S["small_read"], 1)
                            dve.wait_ge(S["ro_ready"], h + 1)
                            o = [psA[:, (n + 2 * h + t) % 4, :] for t in range(NT)]
                            for t in range(NT):
                                b = 12 * h + 6 * t
                                own.step(V.bn_stats(BST[:, b:b + 6], o[t]))
                            own.wait()
                            for t in range(NT):
                                b = 12 * h + 6 * t
                                ins = V.bn_aggr(MV[:, 4 * h + 2 * t:4 * h + 2 * t + 2], BST[:, b:b + 6])
                                ins.then_inc(S["r_var"], 1) if t else own.step(ins)
                            dve.wait_ge(S["r_rstd"], h + 1)
                            for t in range(NT):
                                V.tensor_scalar(rog[:, t, :], o[t], MV[:, 4 * h + 2 * t:4 * h + 2 * t + 1], RRS[:, 2 * h + t:2 * h + t + 1],
                                                ALU.subtract, ALU.mult).then_inc(S["acc_read"], 1)
                            dve.wait_ge(S["acc_read"], n + 2 * h + 2)
                            for t in range(NT):
                                V.tensor_tensor(rog[:, t, :], rog[:, t, :], rg[:, t, h * CH:(h + 1) * CH], ALU.mult).then_inc(S["r_og"], 1)
                            dh, dl = (a_hi, a_lo) if h < 2 else (h_hi, h_lo)
                            k = 4 * (h % 2)
                            cast_rests(m0 + 3 * h + 1, dh[:, k:k + 4, :], dl[:, k:k + 4, :], 2)
                            if h < 2:
                                decay_arg(h + 2)
                    elif name == "final":
                        for t in range(NT):
                            x = Xr[:, t, j * CH:(j + 1) * CH]
                            V.tensor_tensor(x, A[t], x, ALU.add).then_inc(S["x_done"], 1)
                    if s["nu"] and u_tap0 <= s["u"] < u_tap1:
                        taps(taps_total * (s["u"] + s["nu"] - u_tap0) // (u_tap1 - u_tap0))
        clear(nc, S)


def clear(nc, S):
    nums = [s.num for s in S.values()]
    nc.gpsimd.sem_clear(range(min(nums), max(nums) + 1))
    nc.all_engine_barrier()


def persistent(nc, env):
    pb = arena(nc, (nc.sbuf_base + 31) // 32 * 32)
    env["h_hi"] = pb("k_hhi", [P, KT, T], F32R)
    env["h_lo"] = pb("k_hlo", [P, KT, T], F32R)
    env["mod_all"] = pb("k_mod_all", [P, 48 * DEPTH])
    env["base1"] = pb.at[0]
    for name, n in (("i1T", T), ("i2T", T), ("gT", T), ("mod", 48)):
        env[name] = pb("k_" + name, [P, n])
    env["base"] = pb.at[0]


H2 = 8
NE = 128
SLOTS = 128
BIAS_N = 384


def plan_second():
    pl, src = Plan(), []

    def half_units(w, c0):
        for h in (0, 1):
            src.append((w, h * 512, c0, "A"))

    half_units("w_in_2", 0)
    pl.add("q", "A", 0, 2, 2)
    half_units("w_in_2", 512)
    pl.add("kvsu", "A", 0, 2, 2)
    src.append(("w_in_2", 0, 1024, "B"))
    pl.add("sv", "C", 0, 1, 1)
    for i, name in enumerate(("ch", "cc", "cb")):
        src.append(("w_in_2", 0, 1280 + 256 * i, "B"))
        pl.add(name, "B", 0, 1, 1)
    pl.add("mix", "T", slots=5)
    for c in range(2):
        half_units("w_out_2", CH * c)
        pl.add("out", "A", c, 2, 2)
    pl.add("norm2", "T")
    for h in range(8):
        src.append(("peer_wq_2", 0, 256 * h, "B"))
        pl.add("pq", "B", h, 1, 1)
    pl.add("choose", "T")
    assert len(src) == pl.units
    return pl, src


PLAN2, SRC2 = plan_second()
U2 = PLAN2.units
P2 = dict(norm1_g=8, norm2_g=8, gain=8, conv_w=6, sgu_b=4, qg=64, kg=64, sink=8)
P2OFF, P2N = offsets(P2)
ADA_U = 24


def prepare(nc, env, inp):
    x_dram = env["xd"]
    pb = arena(nc, env["base"])
    NRAW = 4
    raw = pb("p_raw", [P, NRAW, UNIT])
    c_in = pb("p_c", [P, KT])
    c_act = pb("p_cact", [P, KT])
    c_tanh = pb("p_ctanh", [P, KT])
    b_ada = pb("p_bada", [P, 48 * DEPTH])
    rel = pb("p_rel", [P, H2])
    pick = pb("p_pick", [P, BIAS_N])
    rows = pb("p_rows", [P, H2, BIAS_N])
    mod_all = env["mod_all"]
    with ExitStack() as cx:
        ps = cx.enter_context(nc.psum_tensor("p_ps", [P, 2, CH], F32))
        psb = cx.enter_context(nc.psum_tensor("p_psb", [P, 4, CH], F32))
        names = "raw0 raw1 raw2 raw3 in_c in_rel x_copied c_tanh_ready c_ready neg_row bias_mm bias_rows bias_out unit_done mod_read mod_ready".split()
        S = {n: cx.enter_context(nc.semaphore("p_" + n)) for n in names}
        with nc.Block() as block:
            groups = DEPTH * ADA_U // NRAW

            @block.sync
            def _(sp):
                sp.dma_start(c_in[:, :], inp["c"]).then_inc(S["in_c"], 16)
                sp.dma_start(b_ada[:, :], inp["b_ada"]).then_inc(S["in_c"], 16)
                sp.dma_start(rel[0:32, :], inp["rel"]).then_inc(S["in_rel"], 16)
                sp.dma_start(pick[0:33, :], inp["pick"]).then_inc(S["in_rel"], 16)

                def load(u, k):
                    sp.dma_start(raw[:, k, :], inp["ada"][bass.ds(u, 1), :, :].rearrange("o p n -> p (o n)")).then_inc(S[f"raw{k}"], 16)

                for k in range(NRAW):
                    load(k, k)
                with sp.Fori(1, groups) as i:
                    for k in range(NRAW):
                        sp.wait_ge(S["unit_done"], i * NRAW + (k + 1 - NRAW))
                        load(i * NRAW + k, k)

            @block.scalar
            def _(act):
                act.dma_start(x_dram, inp["x"]).then_inc(S["x_copied"], 16)
                act.wait_ge(S["in_c"], 32)
                nc.scalar.activation(c_tanh[:, :], c_in[:, :], ACT.Tanh, scale=0.5).then_inc(S["c_tanh_ready"], 1)
                act.wait_ge(S["bias_rows"], 2)
                act.dma_start(env["bias_rows"], rows[:, :, :]).then_inc(S["bias_out"], 16)
                act.wait_ge(S["bias_out"], 16)
                act.wait_ge(S["x_copied"], 16)

            @block.gpsimd
            def _(pool):
                nc.gpsimd.memset(rel[32:33, :], NEG).then_inc(S["neg_row"], 1)

            @block.tensor
            def _(pe):
                pe.wait_ge(S["in_rel"], 32)
                pe.wait_ge(S["neg_row"], 1)
                for half in range(2):
                    if half:
                        pe.wait_ge(S["bias_rows"], 1)
                    for h in range(4):
                        last = nc.tensor.matmul(psb[:, h, 0:BIAS_N], rel[0:33, 4 * half + h:4 * half + h + 1].to_broadcast([33, P]),
                                                pick[0:33, :], start=True, stop=True)
                    last.then_inc(S["bias_mm"], 1)
                pe.wait_ge(S["c_ready"], 1)

                def group(i, bank, first):
                    if not first:
                        pe.wait_ge(S["mod_read"], i - 1)
                    for k in range(NRAW):
                        pe.wait_ge(S[f"raw{k}"], (i + 1) * 16)
                        for f in range(2):
                            for kt in range(KT):
                                last = nc.tensor.matmul(ps[:, bank, 2 * k + f:2 * k + f + 1], raw[:, k, kt * 256 + f * P:kt * 256 + (f + 1) * P],
                                                        c_act[:, kt:kt + 1], start=kt == 0, stop=kt == KT - 1)
                        last.then_inc(S["unit_done"], 1)

                group(0, 0, True)
                group(1, 1, True)
                with pe.Fori(1, groups // 2) as i:
                    for b in range(2):
                        group(i * 2 + b, b, False)

            @block.vector
            def _(dve):
                V = nc.vector
                dve.wait_ge(S["c_tanh_ready"], 1)
                V.scalar_tensor_tensor(c_act[:, :], c_tanh[:, :], 1.0, c_in[:, :], ALU.add, ALU.mult).then_inc(S["mod_ready"], 1)
                dve.wait_ge(S["mod_ready"], 1)
                V.tensor_scalar(c_act[:, :], c_act[:, :], 0.5, None, ALU.mult).then_inc(S["c_ready"], 1)
                for half in range(2):
                    dve.wait_ge(S["bias_mm"], half + 1)
                    V.tensor_copy(rows[:, 4 * half:4 * half + 4, :], psb[:, :, 0:BIAS_N]).then_inc(S["bias_rows"], 1)
                dve.wait_ge(S["in_c"], 32)
                with dve.Fori(0, groups // 2) as i:
                    for b in range(2):
                        dve.wait_ge(S["unit_done"], (i * 2 + b + 1) * NRAW)
                        V.tensor_tensor(mod_all[:, bass.ds(i * 16 + 8 * b, 8)], ps[:, b, 0:8], b_ada[:, bass.ds(i * 16 + 8 * b, 8)],
                                        ALU.add).then_inc(S["mod_read"], 1)
        clear(nc, S)


def second_mixer(nc, env, l, inp):
    x_dram = env["xd"]
    pb = arena(nc, env["base"])
    h_hi, h_lo = env["h_hi"], env["h_lo"]
    Xr = pb("s_x", [P, NT, D])
    ident = pb("s_ident", [P, P])
    iota = pb("s_iota", [P, P])
    caus = pb("s_caus", [P, P])
    PA = pb("s_par", [P, P2N])
    par = {k: PA[:, a:a + n] for k, (a, n) in P2OFF.items()}
    mod = env["mod"]
    SH1, SC1, G1, SH2, SC2 = (mod[:, 8 * i:8 * i + 8] for i in range(5))
    bt = pb("s_bias", [P, H2, T])
    sgw = pb("s_sgw", [P, 4, P])
    keys = pb("s_keys", [P, 16, NE])
    NRAW, NW = 2, 3
    raw = pb("s_raw", [P, NRAW, UNIT])
    w_hi = pb("s_whi", [P, NW, UNIT], F32R)
    w_lo = pb("s_wlo", [P, NW, UNIT], F32R)
    mix_at = pb.at[0]
    a_hi = pb("s_ahi", [P, KT, T], F32R)
    a_lo = pb("s_alo", [P, KT, T], F32R)
    tmp = pb("s_tmp", [P, 4, CH])
    stat = pb("s_stat", [P, 192])
    minus_half = pb("s_mhalf", [P, 8])
    ones = pb("s_ones", [P, P])
    rt = pb("s_rt", [P, T])
    g1 = pb("s_g1", [P, D])
    late_at = pb.at[0]
    qn = pb("s_qn", [P, NT, CH])
    kd = pb("s_kd", [P, NT, 256])
    qT = pb("s_qT", [P, 4, T])
    kT = pb("s_kT", [P, 2, T])
    av = pb("s_av", [P, NT, P])
    su = pb("s_su", [P, NT, 256])
    sv = pb("s_sv", [P, NT, 256])
    ya = pb("s_ya", [P, NT, CH])
    ys = pb("s_ys", [P, NT, 256])
    ch = pb("s_ch", [P, 2, T])
    zp = pb("s_zp", [P, 2, T + 2])
    cy = pb("s_cy", [P, 2, T])
    sm = pb("s_sm", [P, 2, 768])
    pt = pb("s_pt", [P, 2, 384])
    top = pb.at[0]
    pb.at[0] = late_at
    qp = pb("s_qp", [P, 2, 2 * T])
    sc = pb("s_sc", [P, 2, 4, NE])
    sc2 = pb("s_sc2", [P, 2, 4, NE])
    tv = pb("s_tv", [P, NT, 8, 2, 16])
    ti = pb("s_ti", [P, NT, 8, 2, 16], U32)
    tf = pb("s_tf", [P, NT, 8, 2, 16])
    cand = pb("s_cand", [P, 2, NT, 256])
    cand2 = pb("s_cand2", [P, 2, NT, 256])
    bv = pb("s_bv", [P, NT, 8, 16])
    bp = pb("s_bp", [P, NT, 8, 16], U32)
    bx = pb("s_bx", [P, 2, NT * 128], U32)
    bf = pb("s_bf", [P, 2, NT * 128])
    iv = pb("s_iv", [P, 3, NT, 128])
    assert max(top, pb.at[0]) <= nc.sbuf_usable_end, (top, pb.at[0], nc.sbuf_usable_end)
    tmpx = tmp[:, :, :].rearrange("p (t a) n -> p t (a n)", t=NT)
    one_hot = tmp[:, :, :].rearrange("p a (s c) -> p (a s) c", c=16)
    SS, RS, ASS, ARS, NMX, SUM, ES, RDEN, NSINK, GS1, GS2, GSS, GRS, YSS, YRS, SS2, RS2, ESUM = (
        stat[:, a:b] for a, b in ((0, 2), (2, 4), (4, 28), (28, 52), (52, 68), (68, 84), (84, 100), (100, 116),
                                  (116, 124), (124, 132), (132, 140), (140, 148), (148, 156), (156, 160), (160, 164),
                                  (164, 166), (166, 168), (168, 184)))
    with ExitStack() as cx:
        psA = cx.enter_context(nc.psum_tensor("s_psA", [P, 4, CH], F32))
        psS = cx.enter_context(nc.psum_tensor("s_psS", [P, 4, CH], F32))
        names = """in_x in_par in_bias raw0 raw1 hi_ready lo_ready unit_done acc_read small_ready small_read
            dve_step pool_step const_ready mod_here x_sq x_rstd x_norm h_hi_ready h_lo_ready a_sq a_ss a_rstd a_qn
            s_ready s_masked s_negmax s_exp s_sink pt_ready pt_read o_ready y_attn y_sq y_rstd
            g_sq g_ss g_rstd g_vn g_mm c_sq c_sd c_n a_hi_ready y_n w_masked g1_mm
            q_copied t_sub t_exp iv_ready x_done out_x g1_ready""".split()
        S = {n: cx.enter_context(nc.semaphore("s_" + n)) for n in names}
        raw_in = [S["raw0"], S["raw1"]]
        steps = PLAN2.steps
        by = {(s["name"], s["j"]): s for s in steps}
        small, m = {}, 0
        for name, count in (("norm", 4), ("tq", 2), ("tk", 1), ("cmean", 1), ("tm", 3), ("norm2", 4), ("score", 8), ("picks", 3)):
            small[name] = m
            m += count
        n_mix = by[("mix", 0)]["n"]
        n_gate, n_heads = n_mix, n_mix + 1

        with nc.Block() as block:

            @block.sync
            def _(sp):
                sp.dma_start(Xr[:, :, :], x_dram).then_inc(S["in_x"], 16)
                n1 = COFF["iota"][0]
                sp.dma_start(ident[:, :], inp["consts"][:, 0:P]).then_inc(S["in_par"], 16)
                sp.dma_start(iota[:, :], inp["consts"][:, n1:n1 + P]).then_inc(S["in_par"], 16)
                sp.dma_start(caus[:, :], inp["consts"][:, n1 + P:n1 + 2 * P]).then_inc(S["in_par"], 16)
                sp.dma_start(PA[:, :], inp["par2"][bass.ds(l, 1), :, :].rearrange("o p n -> p (o n)")).then_inc(S["in_par"], 16)

                def load(u, k):
                    src = inp["ws2"][bass.ds(l * U2 + u, 1), :, :].rearrange("o p n -> p (o n)")
                    sp.dma_start(raw[:, k, :], src).then_inc(raw_in[k], 16)

                for k in range(NRAW):
                    load(k, k)
                sp.dma_start(sgw[:, :, :].rearrange("p g t -> p (g t)"), inp["sgw"][bass.ds(l, 1), :, :].rearrange("o p n -> p (o n)")).then_inc(S["in_bias"], 16)
                sp.dma_start(keys[:, :, :].rearrange("p g t -> p (g t)"), inp["keys"][bass.ds(l, 1), :, :].rearrange("o p n -> p (o n)")).then_inc(S["in_bias"], 16)
                rows = env["bias_rows"]
                sp.dma_start(bt[:, :, :], bass.AP(rows.tensor, P - 1, [[H2 * BIAS_N - 1, P], [BIAS_N, H2], [1, T]])).then_inc(S["in_bias"], 16)
                with sp.Fori(1, U2 // NRAW) as i:
                    for k in range(NRAW):
                        sp.wait_ge(S["lo_ready"], i * NRAW + (k + 1 - NRAW))
                        load(i * NRAW + k, k)
                sp.wait_ge(S["x_done"], 4)
                sp.dma_start(x_dram, Xr[:, :, :]).then_inc(S["out_x"], 16)
                sp.wait_ge(S["out_x"], 16)

            @block.tensor
            def _(pe):
                pe.wait_ge(S["in_par"], 64)

                def small_bank(i):
                    if i >= 4:
                        pe.wait_ge(S["small_read"], i - 3)
                    return psS[:, i % 4, :]

                def two_tiles(m, tile, ready=None):
                    bank = small_bank(m)
                    for kk in range(2):
                        for t in range(NT):
                            last = nc.tensor.transpose(bank[:, kk * T + t * P:kk * T + (t + 1) * P], tile(kk, t), ident[:, :])
                    last.then_inc(S["small_ready"], 1)

                pe.wait_ge(S["x_norm"], NT)
                for b in range(4):
                    two_tiles(small["norm"] + b, lambda kk, t: tmpx[:, t, (2 * b + kk) * P:(2 * b + kk + 1) * P])
                pe.wait_ge(S["h_lo_ready"], 1)
                for s in steps:
                    name, kind, j, n = s["name"], s["kind"], s["j"], s["n"]
                    if s["ns"] and n + s["ns"] > 4 and kind != "T":
                        if name == "pq" and j >= 4:
                            pe.wait_ge(S["q_copied"], j - 3)
                        else:
                            pe.wait_ge(S["acc_read"], n + s["ns"] - 4)
                    if kind in "BC":
                        u = s["u"]
                        pe.wait_ge(S["lo_ready"], u + 1)
                        wh, wl = w_hi[:, u % NW, :], w_lo[:, u % NW, :]
                        for f in range(2):
                            for kt in range(KT):
                                c = kt * 256
                                if kind == "B":
                                    ops = [(w[:, c + f * P:c + (f + 1) * P], x[:, kt, :]) for w, x in fp32_pieces(wh, wl, h_hi, h_lo)]
                                else:
                                    ops = [(x[:, kt, f * P:(f + 1) * P], w[:, c:c + 256]) for x, w in fp32_pieces(h_hi, h_lo, wh, wl)]
                                for i, (a, b) in enumerate(ops):
                                    last = nc.tensor.matmul(psA[:, n % 4, f * T:(f + 1) * T], a, b,
                                                            start=kt == 0 and i == 0, stop=kt == KT - 1 and i == 2)
                        last.then_inc(S["unit_done"], 1)
                        if name == "pq":
                            if j:
                                peer_scores(j - 1)
                    elif kind == "A":
                        if name == "out":
                            pe.wait_ge(S["small_read"], small["tm"] + 3)
                            pe.wait_ge(S["c_n"], 2)
                        xh, xl = (a_hi, a_lo) if name == "out" else (h_hi, h_lo)
                        for v in range(2):
                            u = s["u"] + v
                            pe.wait_ge(S["lo_ready"], u + 1)
                            wh, wl = w_hi[:, u % NW, :], w_lo[:, u % NW, :]
                            for t in range(NT):
                                for k in range(4):
                                    kt = 4 * v + k
                                    for i, (x, w) in enumerate(fp32_pieces(xh, xl, wh, wl)):
                                        last = nc.tensor.matmul(psA[:, (n + t) % 4, :], x[:, kt, t * P:(t + 1) * P], w[:, k * CH:(k + 1) * CH],
                                                                start=v == 0 and k == 0 and i == 0, stop=v == 1 and k == 3 and i == 2)
                            last.then_inc(S["unit_done"], 1)
                    elif name == "mix":
                        pe.wait_ge(S["a_qn"], 2)
                        for b in range(2):
                            two_tiles(small["tq"] + b, lambda kk, t: qn[:, t, (2 * b + kk) * P:(2 * b + kk + 1) * P])
                        pe.wait_ge(S["a_qn"], 4)
                        two_tiles(small["tk"], lambda kk, t: kd[:, t, kk * P:(kk + 1) * P])
                        bank = small_bank(small["cmean"])
                        pe.wait_ge(S["c_sq"], 1)
                        for k in range(2):
                            last = nc.tensor.matmul(bank[:, 0:T], ones[:, :], ch[:, k, :], start=k == 0, stop=k == 1)
                        last.then_inc(S["small_ready"], 1)
                        pe.wait_ge(S["acc_read"], n_gate - 3)
                        pe.wait_ge(S["g_vn"], 1)
                        pe.wait_ge(S["w_masked"], 1)
                        for t in range(NT):
                            for g in range(4):
                                last = nc.tensor.matmul(psA[:, n_gate % 4, t * 256 + g * 64:t * 256 + (g + 1) * 64], sgw[:, g, :],
                                                        sv[:, t, g * 64:(g + 1) * 64], start=True, stop=True)
                        last.then_inc(S["g_mm"], 1)
                        pe.wait_ge(S["small_read"], small["cmean"] + 1)

                        def scores(p):
                            if p:
                                pe.wait_ge(S["s_masked"], 2 * p)
                            for hh in range(2):
                                r = slice(64 * hh, 64 * hh + 64)
                                nc.tensor.matmul(psS[:, hh, 0:P], qT[r, p, 0:P], kT[r, p // 2, 0:P], start=True, stop=True)
                                last = nc.tensor.matmul(psS[:, hh, P:P + T], qT[r, p, P:T], kT[r, p // 2, :], start=True, stop=True)
                            last.then_inc(S["s_ready"], 1)

                        scores(0)
                        for p in range(4):
                            if p < 3:
                                scores(p + 1)
                            pe.wait_ge(S["s_exp"], p + 1)
                            if p:
                                pe.wait_ge(S["pt_read"], 2 * p)
                            for hh in range(2):
                                for c in range(3):
                                    last = nc.tensor.transpose(psS[:, 2 + hh, c * P:(c + 1) * P], sm[:, p % 2, hh * 384 + c * P:hh * 384 + (c + 1) * P], ident[:, :])
                            last.then_inc(S["pt_ready"], 1)
                            nn = n_heads + p
                            pe.wait_ge(S["acc_read"], nn - 3)
                            pe.wait_ge(S["pt_read"], 2 * p + 2)
                            v = slice((p // 2) * 64, (p // 2) * 64 + 64)
                            for hh in range(2):
                                nc.tensor.matmul(psA[:, nn % 4, hh * 64:hh * 64 + 64], pt[:, hh, 0:P], av[:, 0, v], start=True, stop=True)
                                for jt in range(2):
                                    last = nc.tensor.matmul(psA[:, nn % 4, 128 + hh * 64:128 + hh * 64 + 64], pt[:, hh, (1 + jt) * P:(2 + jt) * P],
                                                            av[:, jt, v], start=jt == 0, stop=jt == 1)
                            last.then_inc(S["o_ready"], 1)
                        pe.wait_ge(S["s_masked"], 8)
                        pe.wait_ge(S["mod_here"], 1)
                        for c in range(KT):
                            last = nc.tensor.matmul(psS[:, c // 4, (c % 4) * P:(c % 4 + 1) * P], G1[:, c:c + 1].to_broadcast([P, P]), ident[:, :],
                                                    start=True, stop=True)
                        last.then_inc(S["g1_mm"], 1)
                        pe.wait_ge(S["g1_ready"], 1)
                        pe.wait_ge(S["y_n"], 4)
                        for b in range(2):
                            two_tiles(small["tm"] + b, lambda kk, t: ya[:, t, (2 * b + kk) * P:(2 * b + kk + 1) * P])
                        two_tiles(small["tm"] + 2, lambda kk, t: ys[:, t, kk * P:(kk + 1) * P])
                    elif name == "norm2":
                        pe.wait_ge(S["x_norm"], 2 * NT)
                        for b in range(4):
                            two_tiles(small["norm2"] + b, lambda kk, t: tmpx[:, t, (2 * b + kk) * P:(2 * b + kk + 1) * P])
                        pe.wait_ge(S["h_lo_ready"], 2)

                        def peer_scores(h):
                            bank = small_bank(small["score"] + h)
                            pe.wait_ge(S["q_copied"], h + 1)
                            for t in range(NT):
                                for k in range(2):
                                    last = nc.tensor.matmul(bank[:, (2 * t + k) * NE:(2 * t + k + 1) * NE], qp[:, h % 2, k * T + t * P:k * T + (t + 1) * P],
                                                            keys[:, 2 * h + k, :], start=True, stop=True)
                            last.then_inc(S["small_ready"], 1)
                    elif name == "choose":
                        peer_scores(7)
                        pe.wait_ge(S["iv_ready"], 1)
                        for i in range(3):
                            bank = small_bank(small["picks"] + i)
                            for t in range(NT):
                                last = nc.tensor.transpose(bank[:, t * P:(t + 1) * P], iv[:, i, t, :], ident[:, :])
                            last.then_inc(S["small_ready"], 1)

            @block.scalar
            def _(act):
                converted = [0]

                def heads(upto):
                    while converted[0] <= min(upto, U2 - 1):
                        u = converted[0]
                        act.wait_ge(raw_in[u % NRAW], 16 * (u // NRAW + 1))
                        if u >= NW:
                            act.wait_ge(S["unit_done"], u - NW + 1)
                        nc.scalar.activation(w_hi[:, u % NW, :], raw[:, u % NRAW, :], ACT.Copy).then_inc(S["hi_ready"], 1)
                        converted[0] += 1

                def h_heads(first, gain, shift):
                    for kt in range(KT):
                        act.wait_ge(S["small_ready"], first + kt // 2 + 1)
                        nc.scalar.activation(h_hi[:, kt, :], psS[:, (first + kt // 2) % 4, (kt % 2) * T:(kt % 2 + 1) * T], ACT.Identity,
                                             scale=gain[:, kt:kt + 1], bias=shift[:, kt:kt + 1]).then_inc(S["h_hi_ready"], 1)

                act.wait_ge(S["in_x"], 16)
                for t in range(NT):
                    nc.scalar.activation(g1[:, :], Xr[:, t, :], ACT.Square, accum_out=SS[:, t:t + 1]).then_inc(S["x_sq"], 1)
                    act.wait_ge(S["x_sq"], t + 1)
                act.wait_ge(S["in_par"], 64)
                heads(2)
                act.wait_ge(S["mod_here"], 1)
                h_heads(small["norm"], GS1, SH1)
                for s in steps:
                    name, j, n = s["name"], s["j"], s["n"]
                    if s["nu"]:
                        heads(s["u"] + s["nu"] + 1)
                    if name in ("q", "kvsu"):
                        act.wait_ge(S["unit_done"], s["u"] + s["nu"])
                        w = CH if name == "q" else P
                        for t in range(NT):
                            i = (0 if name == "q" else 2) + t
                            nc.scalar.activation(tmp[:, i, 0:w], psA[:, (n + t) % 4, 0:w], ACT.Square).then_inc(S["a_sq"], 1)
                    elif name == "mix":
                        act.wait_ge(S["acc_read"], by[("sv", 0)]["n"] + 1)
                        nc.scalar.activation(tmp[:, 0, :], sv[:, :, :].rearrange("p t n -> p (t n)"), ACT.Square).then_inc(S["g_sq"], 1)
                        act.wait_ge(S["acc_read"], by[("cb", 0)]["n"] + 1)
                        nc.scalar.activation(ch[:, :, :], cy[:, :, :], ACT.Square).then_inc(S["c_sq"], 1)
                        act.wait_ge(S["small_read"], small["cmean"] + 1)
                        nc.scalar.activation(rt[:, :], rt[:, :], ACT.Sqrt).then_inc(S["c_sd"], 1)

                        def exps(p):
                            act.wait_ge(S["s_negmax"], p + 1)
                            for t in range(NT):
                                for hh in range(2):
                                    row = sm[:, p % 2, hh * 384:hh * 384 + P] if t == 0 else sm[:, p % 2, hh * 384 + P:hh * 384 + 384]
                                    c = 4 * p + 2 * t + hh
                                    ins = nc.scalar.activation(row, row, ACT.Exp, bias=NMX[:, c:c + 1], accum_out=SUM[:, c:c + 1])
                            ins.then_inc(S["s_exp"], 1)
                            for hh in range(2):
                                c = slice(4 * p + hh, 4 * p + hh + 3, 2)
                                ins = nc.scalar.activation(ES[:, c], NMX[:, c], ACT.Exp, bias=par["sink"][:, 2 * p + hh:2 * p + hh + 1])
                            ins.then_inc(S["s_sink"], 1)

                        exps(0)
                        for p in range(4):
                            if p < 3:
                                exps(p + 1)
                            act.wait_ge(S["pt_ready"], p + 1)
                            if p:
                                act.wait_ge(S["o_ready"], p)
                            for hh in range(2):
                                nc.scalar.activation(pt[:, hh, :], psS[:, 2 + hh, 0:384], ACT.Copy).then_inc(S["pt_read"], 1)
                        act.wait_ge(S["c_n"], 1)
                        for k in range(2):
                            nc.scalar.activation(a_hi[:, 4 + k, :], cy[:, k, :], ACT.Copy, scale=par["gain"][:, 4 + k:5 + k]).then_inc(S["a_hi_ready"], 1)
                        act.wait_ge(S["acc_read"], n_gate + 1)
                        for t in range(NT):
                            nc.scalar.activation(tmp[:, 2 + t, 0:256], ys[:, t, :], ACT.Square, accum_out=YSS[:, 2 + t:3 + t]).then_inc(S["y_sq"], 1)
                        act.wait_ge(S["acc_read"], n_heads + 4)
                        for t in range(NT):
                            nc.scalar.activation(tmp[:, t, :], ya[:, t, :], ACT.Square, accum_out=YSS[:, t:t + 1]).then_inc(S["y_sq"], 1)
                        for i in range(3):
                            act.wait_ge(S["small_ready"], small["tm"] + i + 1)
                            for kk in range(2):
                                kt = (0, 2, 6)[i] + kk
                                nc.scalar.activation(a_hi[:, kt, :], psS[:, (small["tm"] + i) % 4, kk * T:(kk + 1) * T], ACT.Copy,
                                                     scale=par["gain"][:, kt:kt + 1]).then_inc(S["a_hi_ready"], 1)
                    elif name == "norm2":
                        act.wait_ge(S["x_done"], 4)
                        for t in range(NT):
                            nc.scalar.activation(g1[:, :], Xr[:, t, :], ACT.Square, accum_out=SS2[:, t:t + 1]).then_inc(S["x_sq"], 1)
                            act.wait_ge(S["x_sq"], 3 + t)
                        h_heads(small["norm2"], GS2, SH2)
                    elif name == "pq":
                        act.wait_ge(S["unit_done"], s["u"] + 1)
                        if j >= 2:
                            act.wait_ge(S["small_ready"], small["score"] + j - 1)
                        nc.scalar.activation(qp[:, j % 2, :], psA[:, n % 4, :], ACT.Copy).then_inc(S["q_copied"], 1)
                    elif name == "choose":
                        act.wait_ge(S["t_sub"], 1)
                        nc.scalar.activation(iv[:, 2, :, :], iv[:, 2, :, :], ACT.Exp).then_inc(S["t_exp"], 1)

            @block.gpsimd
            def _(pool):
                own = Steps(pool, S["pool_step"])

                def rstd(dst, src, width, scale, done):
                    own.link(nc.gpsimd.tensor_scalar(dst, src, scale, EPS, ALU.mult, ALU.add))
                    nc.gpsimd.tensor_tensor(dst, dst, minus_half[:, 0:width], ALU.pow).then_inc(done, 1)

                own.step(nc.gpsimd.memset(minus_half[:, :], -0.5))
                nc.gpsimd.memset(ones[:, :], 1.0 / 256).then_inc(S["const_ready"], 1)
                nc.gpsimd.memset(zp[:, :, 0:2], 0.0).then_inc(S["const_ready"], 1)
                own.wait()
                pool.wait_ge(S["x_sq"], NT)
                rstd(RS, SS, NT, 1.0 / D, S["x_rstd"])
                for i in range(4):
                    pool.wait_ge(S["a_ss"], i + 1)
                    w = 8 if i < 2 else 2
                    rstd(ARS[:, 8 * i - 6 * max(0, i - 2):8 * i - 6 * max(0, i - 2) + w], ASS[:, 8 * i - 6 * max(0, i - 2):8 * i - 6 * max(0, i - 2) + w],
                         w, 1.0 / 64, S["a_rstd"])
                pool.wait_ge(S["g_ss"], 1)
                rstd(GRS, GSS, 8, 1.0 / 64, S["g_rstd"])
                pool.wait_ge(S["y_sq"], 2)
                rstd(YRS[:, 2:4], YSS[:, 2:4], 2, 1.0 / 256, S["y_rstd"])
                pool.wait_ge(S["y_sq"], 4)
                rstd(YRS[:, 0:2], YSS[:, 0:2], 2, 1.0 / 512, S["y_rstd"])
                pool.wait_ge(S["x_sq"], 2 * NT)
                rstd(RS2, SS2, NT, 1.0 / D, S["x_rstd"])

            @block.vector
            def _(dve):
                own = Steps(dve, S["dve_step"])
                V = nc.vector
                converted = [0]

                def rests(upto):
                    while converted[0] <= min(upto, U2 - 1):
                        u = converted[0]
                        dve.wait_ge(S["hi_ready"], u + 1)
                        V.tensor_tensor(w_lo[:, u % NW, :], raw[:, u % NRAW, :], w_hi[:, u % NW, :].bitcast(F32),
                                        ALU.subtract).then_inc(S["lo_ready"], 1)
                        converted[0] += 1

                def h_rests(first, gain, shift, done):
                    for kt in range(KT):
                        dve.wait_ge(S["h_hi_ready"], done + kt - kt % 2 + 2)
                        v = tmp2[:, kt % 4, :]
                        ins = V.tensor_scalar(v, psS[:, (first + kt // 2) % 4, (kt % 2) * T:(kt % 2 + 1) * T], gain[:, kt:kt + 1],
                                              shift[:, kt:kt + 1], ALU.mult, ALU.add)
                        if kt % 2:
                            ins.then_inc(S["small_read"], 1)
                            dve.wait_ge(S["small_read"], first + kt // 2 + 1)
                        else:
                            own.link(ins)
                        ins = V.tensor_tensor(h_lo[:, kt, :], v, h_hi[:, kt, :].bitcast(F32), ALU.subtract)
                        ins.then_inc(S["h_lo_ready"], 1) if kt == KT - 1 else own.step(ins)

                def x_norm(rs):
                    for t in range(NT):
                        V.tensor_scalar(tmpx[:, t, :], Xr[:, t, :], rs[:, t:t + 1], None, ALU.mult).then_inc(S["x_norm"], 1)

                tmp2 = sm[:, :, :].rearrange("p a n -> p (a n)")[:, 0:1024].rearrange("p (a n) -> p a n", a=4)

                dve.wait_ge(S["in_par"], 64)
                own.link(V.tensor_copy(mod[:, :], env["mod_all"][:, bass.ds(l * 48, 48)]))
                own.link(V.tensor_scalar(GS1, SC1, 1.0, None, ALU.add))
                own.link(V.tensor_scalar(GS2, SC2, 1.0, None, ALU.add))
                own.step(V.tensor_scalar(par["qg"], par["qg"], 0.125, None, ALU.mult))
                own.step(V.tensor_scalar(NSINK, par["sink"], -1.0, None, ALU.mult))
                own.link(V.tensor_tensor(GS2, GS2, par["norm2_g"], ALU.mult))
                V.tensor_tensor(GS1, GS1, par["norm1_g"], ALU.mult).then_inc(S["mod_here"], 1)
                dve.wait_ge(S["mod_here"], 1)
                dve.wait_ge(S["in_bias"], 48)
                V.tensor_tensor(sgw[:, :, :], sgw[:, :, :], caus[:, :].rearrange("p (a n) -> p a n", a=1).to_broadcast([P, 4, P]),
                                ALU.mult).then_inc(S["w_masked"], 1)
                dve.wait_ge(S["x_rstd"], 1)
                x_norm(RS)
                rests(2)
                h_rests(small["norm"], GS1, SH1, 0)
                for s in steps:
                    name, j, n = s["name"], s["j"], s["n"]
                    if s["nu"]:
                        rests(s["u"] + s["nu"] + 1)
                        if name != "pq":
                            dve.wait_ge(S["unit_done"], s["u"] + s["nu"])
                    A = [psA[:, (n + t) % 4, :] for t in range(NT)]
                    if name in ("q", "kvsu"):
                        nh = 8 if name == "q" else 2
                        i0 = 0 if name == "q" else 2
                        at = (0, 8, 16, 18)
                        for t in range(NT):
                            dve.wait_ge(S["a_sq"], i0 + t + 1)
                            V.tensor_reduce(ASS[:, at[i0 + t]:at[i0 + t] + nh], tmp[:, i0 + t, 0:nh * 64].rearrange("p (h n) -> p h n", n=64),
                                            AX.X, ALU.add).then_inc(S["a_ss"], 1)
                        for t in range(NT):
                            i = i0 + t
                            gain = (par["qg"] if nh == 8 else par["kg"]).rearrange("p (h n) -> p h n", h=1).to_broadcast([P, nh, 64])
                            if nh == 8:
                                x = qn[:, t, :].rearrange("p (h n) -> p h n", n=64)
                            else:
                                kx = kd[:, t, :].rearrange("p (h c n) -> p h c n", c=2, n=64)
                                x = kx[:, :, 0, :]
                                own.step(V.tensor_copy(av[:, t, :], A[t][:, P:2 * P]))
                                own.step(V.tensor_copy(su[:, t, :], A[t][:, 256:512]))
                            dve.wait_ge(S["a_rstd"], i + 1)
                            r = ARS[:, at[i]:at[i] + nh].rearrange("p (h n) -> p h n", n=1).to_broadcast([P, nh, 64])
                            V.tensor_tensor(x, A[t][:, 0:nh * 64].rearrange("p (h n) -> p h n", n=64), r, ALU.mult).then_inc(S["acc_read"], 1)
                            dve.wait_ge(S["acc_read"], n + t + 1)
                            ins = V.tensor_tensor(x, x, gain, ALU.mult)
                            if nh == 8:
                                ins.then_inc(S["a_qn"], 1)
                            else:
                                own.link(ins)
                                V.tensor_copy(kx[:, :, 1, :], x).then_inc(S["a_qn"], 1)
                    elif name == "sv":
                        x = A[0].rearrange("p (g n) -> p g n", n=64)
                        own.link(V.tensor_reduce(GSS, x, AX.X, ALU.add))
                        own.link(V.tensor_scalar(GSS, GSS, 1.0 / 64, None, ALU.mult))
                        V.tensor_tensor(sv[:, :, :].rearrange("p t (g n) -> p (t g) n", n=64), x,
                                        GSS.rearrange("p (g n) -> p g n", n=1).to_broadcast([P, 8, 64]), ALU.subtract).then_inc(S["acc_read"], 1)
                        dve.wait_ge(S["acc_read"], n + 1)
                    elif name == "ch":
                        V.tensor_copy(ch[:, :, :].rearrange("p a n -> p (a n)"), A[0]).then_inc(S["acc_read"], 1)
                        dve.wait_ge(S["acc_read"], n + 1)
                    elif name == "cc":
                        dve.wait_ge(S["const_ready"], 2)
                        V.tensor_tensor(zp[:, :, 2:T + 2], A[0].rearrange("p (a n) -> p a n", a=2), ch[:, :, :], ALU.mult).then_inc(S["acc_read"], 1)
                        dve.wait_ge(S["acc_read"], n + 1)
                        for tap in range(3):
                            for f in range(2):
                                w = par["conv_w"][:, 3 * f + tap:3 * f + tap + 1]
                                if tap == 0:
                                    own.step(V.tensor_scalar(cy[:, f, :], zp[:, f, 0:T], w, None, ALU.mult))
                                else:
                                    own.wait(own.n - 1)
                                    own.step(V.scalar_tensor_tensor(cy[:, f, :], zp[:, f, tap:tap + T], w, cy[:, f, :], ALU.mult, ALU.add))
                        own.wait()
                    elif name == "cb":
                        y = cy[:, :, :].rearrange("p a n -> p (a n)")
                        V.tensor_tensor(y, A[0], y, ALU.mult).then_inc(S["acc_read"], 1)
                    elif name == "mix":
                        dve.wait_ge(S["g_sq"], 1)
                        V.tensor_reduce(GSS, tmp[:, 0, :].rearrange("p (g n) -> p g n", n=64), AX.X, ALU.add).then_inc(S["g_ss"], 1)
                        for b in range(2):
                            dve.wait_ge(S["small_ready"], small["tq"] + b + 1)
                            V.tensor_copy(qT[:, 2 * b:2 * b + 2, :].rearrange("p a n -> p (a n)"), psS[:, (small["tq"] + b) % 4, :]).then_inc(S["small_read"], 1)
                        dve.wait_ge(S["small_ready"], small["tk"] + 1)
                        V.tensor_copy(kT[:, :, :].rearrange("p a n -> p (a n)"), psS[:, small["tk"] % 4, :]).then_inc(S["small_read"], 1)
                        dve.wait_ge(S["small_ready"], small["cmean"] + 1)
                        V.tensor_scalar(rt[:, :], psS[:, small["cmean"] % 4, 0:T], EPS, None, ALU.add).then_inc(S["small_read"], 1)
                        dve.wait_ge(S["g_rstd"], 1)
                        x = sv[:, :, :].rearrange("p t (g n) -> p (t g) n", n=64)
                        V.tensor_tensor(x, x, GRS.rearrange("p (g n) -> p g n", n=1).to_broadcast([P, 8, 64]), ALU.mult).then_inc(S["g_vn"], 1)
                        dve.wait_ge(S["c_sd"], 1)
                        own.link(V.reciprocal(rt[:, :], rt[:, :]))
                        V.tensor_tensor(cy[:, :, :], cy[:, :, :], rt[:, :].rearrange("p (a n) -> p a n", a=1).to_broadcast([P, 2, T]), ALU.mult).then_inc(S["c_n"], 1)
                        dve.wait_ge(S["g_mm"], 1)
                        mixed = psA[:, n_gate % 4, :].rearrange("p (t n) -> p t n", t=NT)
                        for g in range(4):
                            c = slice(g * 64, (g + 1) * 64)
                            ins = V.scalar_tensor_tensor(ys[:, :, c], mixed[:, :, c], par["sgu_b"][:, g:g + 1], su[:, :, c], ALU.add, ALU.mult)
                            ins.then_inc(S["acc_read"], 1) if g == 3 else own.step(ins)

                        def masked(p):
                            dve.wait_ge(S["s_ready"], p + 1)
                            if p >= 2:
                                dve.wait_ge(S["pt_ready"], p - 1)
                            s2 = sm[:, p % 2, :].rearrange("p (h n) -> p h n", h=2)
                            V.tensor_tensor(s2[:, :, 0:P], psS[:, 0:2, 0:P], bt[:, 2 * p:2 * p + 2, P:T], ALU.add).then_inc(S["s_masked"], 1)
                            V.tensor_tensor(s2[:, :, P:384], psS[:, 0:2, P:384], bt[:, 2 * p:2 * p + 2, :], ALU.add).then_inc(S["s_masked"], 1)
                            dve.wait_ge(S["s_masked"], 2 * p + 2)
                            nm = NMX[:, 4 * p:4 * p + 4]
                            own.step(V.tensor_reduce(nm[:, 0:2], s2[:, :, 0:P], AX.X, ALU.max, negate=True))
                            own.link(V.tensor_reduce(nm[:, 2:4], s2[:, :, P:384], AX.X, ALU.max, negate=True))
                            nm2 = nm.rearrange("p (t h) -> p t h", t=NT)
                            ns = NSINK[:, 2 * p:2 * p + 2].rearrange("p (t h) -> p t h", t=1).to_broadcast([P, NT, 2])
                            V.tensor_tensor(nm2, nm2, ns, ALU.min).then_inc(S["s_negmax"], 1)

                        masked(0)
                        for p in range(4):
                            if p < 3:
                                masked(p + 1)
                            c = slice(4 * p, 4 * p + 4)
                            dve.wait_ge(S["s_sink"], p + 1)
                            own.link(V.tensor_tensor(RDEN[:, c], SUM[:, c], ES[:, c], ALU.add))
                            own.link(V.reciprocal(RDEN[:, c], RDEN[:, c]))
                            dve.wait_ge(S["o_ready"], p + 1)
                            o = psA[:, (n_heads + p) % 4, 0:256].rearrange("p (t h n) -> p t h n", t=NT, h=2)
                            r = RDEN[:, c].rearrange("p (t h n) -> p t h n", t=NT, n=1).to_broadcast([P, NT, 2, 64])
                            V.tensor_tensor(ya[:, :, 2 * p * 64:(2 * p + 2) * 64].rearrange("p t (h n) -> p t h n", h=2), o, r,
                                            ALU.mult).then_inc(S["acc_read"], 1)
                        dve.wait_ge(S["g1_mm"], 1)
                        dve.wait_ge(S["x_sq"], 2)
                        V.tensor_copy(g1[:, :].rearrange("p (a n) -> p a n", a=2), psS[:, 0:2, :]).then_inc(S["g1_ready"], 1)
                        for k in range(2):
                            dve.wait_ge(S["a_hi_ready"], k + 1)
                            ins = V.scalar_tensor_tensor(a_lo[:, 4 + k, :], cy[:, k, :], par["gain"][:, 4 + k:5 + k], a_hi[:, 4 + k, :].bitcast(F32),
                                                         ALU.mult, ALU.subtract)
                            ins.then_inc(S["c_n"], 1) if k else own.step(ins)
                        for half, (y, c) in enumerate(((ys, 2), (ya, 0))):
                            dve.wait_ge(S["y_rstd"], half + 1)
                            for t in range(NT):
                                V.tensor_scalar(y[:, t, :], y[:, t, :], YRS[:, c + t:c + t + 1], None, ALU.mult).then_inc(S["y_n"], 1)
                        for i in range(3):
                            dve.wait_ge(S["a_hi_ready"], 4 + 2 * i)
                            for kk in range(2):
                                kt = (0, 2, 6)[i] + kk
                                ins = V.scalar_tensor_tensor(a_lo[:, kt, :], psS[:, (small["tm"] + i) % 4, kk * T:(kk + 1) * T], par["gain"][:, kt:kt + 1],
                                                             a_hi[:, kt, :].bitcast(F32), ALU.mult, ALU.subtract)
                                ins.then_inc(S["small_read"], 1) if kk else own.step(ins)
                    elif name == "out":
                        for t in range(NT):
                            c = slice(j * CH, (j + 1) * CH)
                            w = tmp[:, 2 * j + t, :]
                            V.tensor_tensor(w, A[t], g1[:, c], ALU.mult).then_inc(S["acc_read"], 1)
                            dve.wait_ge(S["acc_read"], n + t + 1)
                            V.tensor_tensor(Xr[:, t, c], Xr[:, t, c], w, ALU.add).then_inc(S["x_done"], 1)
                    elif name == "norm2":
                        dve.wait_ge(S["x_rstd"], 2)
                        x_norm(RS2)
                        h_rests(small["norm2"], GS2, SH2, KT)
                    elif name == "pq" and j >= 1:
                        choose(j - 1)
                    elif name == "choose":
                        choose(7)
                        pick()
                    if name == "norm2":

                        def choose(h):
                            b = h % 2
                            m = small["score"] + h
                            dve.wait_ge(S["small_ready"], m + 1)
                            V.tensor_copy(sc[:, b, :, :].rearrange("p a n -> p (a n)"), psS[:, m % 4, :]).then_inc(S["small_read"], 1)
                            dve.wait_ge(S["small_read"], m + 1)
                            rows_ = [(t, k) for t in range(NT) for k in range(2)]
                            for t, k in rows_:
                                own.step(V.max(tv[:, t, h, k, 0:8], sc[:, b, 2 * t + k, :]))
                            own.wait()
                            for t, k in rows_:
                                own.step(V.max_index(ti[:, t, h, k, 0:8], tv[:, t, h, k, 0:8], sc[:, b, 2 * t + k, :]))
                                own.step(V.match_replace(sc2[:, b, 2 * t + k, :], tv[:, t, h, k, 0:8], sc[:, b, 2 * t + k, :], -3.0e38))
                            own.wait()
                            for t, k in rows_:
                                own.step(V.max(tv[:, t, h, k, 8:16], sc2[:, b, 2 * t + k, :]))
                            own.wait()
                            for t, k in rows_:
                                own.step(V.max_index(ti[:, t, h, k, 8:16], tv[:, t, h, k, 8:16], sc2[:, b, 2 * t + k, :]))
                            for t in range(NT):
                                first = tv[:, t, h, 0, :].rearrange("p (a c) -> p a c", c=1).to_broadcast([P, 16, 16])
                                second = tv[:, t, h, 1, :].rearrange("p (a c) -> p a c", a=1).to_broadcast([P, 16, 16])
                                own.step(V.tensor_tensor(cand[:, b, t, :].rearrange("p (a c) -> p a c", a=16), first, second, ALU.add))
                            own.wait()
                            for t in range(NT):
                                own.step(V.max(bv[:, t, h, 0:8], cand[:, b, t, :]))
                            own.wait()
                            for t in range(NT):
                                own.step(V.max_index(bp[:, t, h, 0:8], bv[:, t, h, 0:8], cand[:, b, t, :]))
                                own.step(V.match_replace(cand2[:, b, t, :], bv[:, t, h, 0:8], cand[:, b, t, :], -3.0e38))
                            own.wait()
                            for t in range(NT):
                                own.step(V.max(bv[:, t, h, 8:16], cand2[:, b, t, :]))
                            own.wait()
                            for t in range(NT):
                                own.step(V.max_index(bp[:, t, h, 8:16], bv[:, t, h, 8:16], cand2[:, b, t, :]))

                        def pick():
                            own.wait()
                            best = bv[:, :, :, :].rearrange("p t h s -> p (t h) s")
                            e = iv[:, 2, :, :].rearrange("p t (h s) -> p (t h) s", s=16)
                            V.tensor_tensor(e, best, best[:, :, 0:1].to_broadcast([P, 16, 16]), ALU.subtract).then_inc(S["t_sub"], 1)
                            pos = bp[:, :, :, :].rearrange("p t h s -> p (t h s)")
                            own.step(V.tensor_scalar(bx[:, 0, :], pos, 4, None, ALU.logical_shift_right))
                            own.step(V.tensor_scalar(bx[:, 1, :], pos, 15, None, ALU.bitwise_and))
                            own.step(V.tensor_copy(tf[:, :, :, :, :].rearrange("p t h k s -> p (t h k s)"), ti[:, :, :, :, :].rearrange("p t h k s -> p (t h k s)")))
                            own.wait()
                            own.link(V.tensor_copy(bf[:, :, :].rearrange("p k n -> p (k n)"), bx[:, :, :].rearrange("p k n -> p (k n)")))
                            for k in range(2):
                                for t in range(NT):
                                    which = bf[:, k, t * 128:(t + 1) * 128].rearrange("p (s c) -> p s c", c=1).to_broadcast([P, 128, 16])
                                    places = iota[:, 0:16].rearrange("p (s c) -> p s c", s=1).to_broadcast([P, 128, 16])
                                    own.link(V.tensor_tensor(one_hot, which, places, ALU.is_equal))
                                    numbers = tf[:, t, :, k, :].rearrange("p h (s c) -> p h s c", s=1).to_broadcast([P, 8, 16, 16])
                                    hot4 = one_hot.rearrange("p (h s) c -> p h s c", h=8)
                                    own.link(V.tensor_tensor(hot4, hot4, numbers, ALU.mult))
                                    own.link(V.tensor_reduce(iv[:, k, t, :], one_hot, AX.X, ALU.add))
                            dve.wait_ge(S["t_exp"], 1)
                            own.link(V.tensor_reduce(ESUM, e, AX.X, ALU.add))
                            own.link(V.reciprocal(ESUM, ESUM))
                            V.tensor_tensor(e, e, ESUM.rearrange("p (a c) -> p a c", c=1).to_broadcast([P, 16, 16]), ALU.mult).then_inc(S["iv_ready"], 1)
                            for i, dst in enumerate((env["i1T"], env["i2T"], env["gT"])):
                                m = small["picks"] + i
                                dve.wait_ge(S["small_ready"], m + 1)
                                V.tensor_copy(dst[:, :], psS[:, m % 4, 0:T]).then_inc(S["small_read"], 1)
        clear(nc, S)


def peer(nc, env, l, inp):
    x_dram = env["xd"]
    pb = arena(nc, env["base"])
    h_hi, h_lo, mod = env["h_hi"], env["h_lo"], env["mod"]
    i1T, i2T, gT = env["i1T"], env["i2T"], env["gT"]
    W = pb("e_w", [P, NE, T])
    ident = pb("e_ident", [P, P])
    iota = pb("e_iota", [P, P])
    gact = pb("e_gact", [P, 2, T])
    g_hi = pb("e_ghi", [P, 2, T], F32R)
    g_lo = pb("e_glo", [P, 2, T], F32R)
    raw_at = pb.at[0]
    raw_d = pb("e_rawd", [P, 2, D])
    raw_u = pb("e_rawu", [P, 2, D])
    hi_d = pb("e_hid", [P, 2, D], F32R)
    hi_u = pb("e_hiu", [P, 2, D], F32R)
    lo_at = pb.at[0]
    lo_d = pb("e_lod", [P, 2, D], F32R)
    lo_u_at = pb.at[0]
    lo_u = pb("e_lou", [P, 2, D], F32R)
    assert pb.at[0] <= nc.sbuf_usable_end, (pb.at[0], nc.sbuf_usable_end)
    hot1 = pb("e_hot1", [P, 2, 4, NE], offset=lo_u_at)
    hot2 = pb("e_hot2", [P, 2, 4, NE], offset=lo_u_at + 4096)
    Xr = pb("e_x", [P, NT, D], offset=raw_at)
    gate = pb("e_gate", [P, D], offset=raw_at + 8192)
    prod = pb("e_prod", [P, NT, D], offset=lo_at)
    GROUP = 4
    with ExitStack() as cx:
        psW = cx.enter_context(nc.psum_tensor("e_psW", [P, 2, CH], F32))
        psD = cx.enter_context(nc.psum_tensor("e_psD", [P, 2, CH], F32))
        psY = cx.enter_context(nc.psum_tensor("e_psY", [P, 4, CH], F32))
        names = """in_const raw_d0 raw_d1 raw_u0 raw_u1 in_x out_x hot1_ready hot2_ready w_mm w_copied
            hi_d_ready lo_d_ready hi_u_ready lo_u_ready down_done gelu_done weighted g_hi_ready g_lo_ready up_done
            gate_mm gate_ready prod_done x_done""".split()
        S = {n: cx.enter_context(nc.semaphore("e_" + n)) for n in names}
        in_d, in_u = [S["raw_d0"], S["raw_d1"]], [S["raw_u0"], S["raw_u1"]]
        pairs = NE // 2

        with nc.Block() as block:

            @block.sync
            def _(sp):
                n1 = COFF["iota"][0]
                sp.dma_start(ident[:, :], inp["consts"][:, 0:P]).then_inc(S["in_const"], 16)
                sp.dma_start(iota[:, :], inp["consts"][:, n1:n1 + P]).then_inc(S["in_const"], 16)

                def load(x, b):
                    sp.dma_start(raw_d[:, b, :], inp["down"][bass.ds(l * NE + x, 1), :, :].rearrange("o p n -> p (o n)")).then_inc(in_d[b], 16)

                def load_up(x, b):
                    sp.dma_start(raw_u[:, b, :], inp["up"][bass.ds(l * NE + x, 1), :, :].rearrange("o p n -> p (o n)")).then_inc(in_u[b], 16)

                for b in range(2):
                    load(b, b)
                    load_up(b, b)
                with sp.Fori(1, pairs) as i:
                    for b in range(2):
                        sp.wait_ge(S["lo_d_ready"], i * 2 + (b - 1))
                        load(i * 2 + b, b)
                        sp.wait_ge(S["lo_u_ready"], i * 2 + (b - 1))
                        load_up(i * 2 + b, b)
                sp.wait_ge(S["lo_d_ready"], NE)
                sp.dma_start(Xr[:, :, :], x_dram).then_inc(S["in_x"], 16)
                sp.wait_ge(S["x_done"], 4)
                sp.dma_start(x_dram, Xr[:, :, :]).then_inc(S["out_x"], 16)
                sp.wait_ge(S["out_x"], 16)

            @block.tensor
            def _(pe):

                def gates(i, g, first):
                    pe.wait_ge(S["hot1_ready"], i * 2 + (g + 1))
                    pe.wait_ge(S["hot2_ready"], i * 2 + (g + 1))
                    if not first:
                        pe.wait_ge(S["w_copied"], i * 2 + (g - 1))
                    for k in range(GROUP):
                        last = nc.tensor.matmul(psW[:, g, k * NE:(k + 1) * NE], hot2[:, g, k, :], hot1[:, g, k, :], start=True, stop=True)
                    last.then_inc(S["w_mm"], 1)

                for g in range(2):
                    gates(0, g, True)
                with pe.Fori(1, T // (2 * GROUP)) as i:
                    for g in range(2):
                        gates(i, g, False)
                pe.wait_ge(S["in_const"], 32)
                pe.wait_ge(S["w_copied"], T // GROUP)
                for c in range(KT):
                    last = nc.tensor.matmul(psW[:, c // 4, (c % 4) * P:(c % 4 + 1) * P], mod[:, 40 + c:41 + c].to_broadcast([P, P]), ident[:, :],
                                            start=True, stop=True)
                last.then_inc(S["gate_mm"], 1)

                def down(x, b, first):
                    pe.wait_ge(S["lo_d_ready"], x + 1)
                    if not first:
                        pe.wait_ge(S["gelu_done"], x - 1)
                    for kt in range(KT):
                        c = slice(kt * P, (kt + 1) * P)
                        for i, (w, h) in enumerate(fp32_pieces(hi_d[:, b, c], lo_d[:, b, c], h_hi[:, kt, :], h_lo[:, kt, :])):
                            last = nc.tensor.matmul(psD[:, b, 0:T], w, h, start=kt == 0 and i == 0, stop=kt == KT - 1 and i == 2)
                    last.then_inc(S["down_done"], 1)

                def up(x, b, start=False, stop=False):
                    pe.wait_ge(S["lo_u_ready"], x + 1)
                    pe.wait_ge(S["g_lo_ready"], x + 1)
                    for t in range(NT):
                        tok = slice(t * P, (t + 1) * P)
                        for i, g, w in ((0, g_hi, hi_u), (1, g_hi, lo_u), (2, g_lo, hi_u)):
                            for c in range(2):
                                last = nc.tensor.matmul(psY[:, 2 * t + c, :], g[:, b, tok], w[:, b, c * CH:(c + 1) * CH],
                                                        start=start and i == 0, stop=stop and i == 2)
                    last.then_inc(S["up_done"], 1)

                down(0, 0, True)
                down(1, 1, True)
                up(0, 0, start=True)
                down(2, 0, False)
                up(1, 1)
                with pe.Fori(1, pairs - 1) as i:
                    for b in range(2):
                        down(i * 2 + (b + 1), 1 - b, False)
                        up(i * 2 + b, b)
                down(NE - 1, 1, False)
                up(NE - 2, 0)
                up(NE - 1, 1, stop=True)

            @block.scalar
            def _(act):

                def to_w(i, g):
                    act.wait_ge(S["w_mm"], i * 2 + (g + 1))
                    nc.scalar.activation(W[:, :, bass.ds(i * (2 * GROUP) + g * GROUP, GROUP)], psW[:, g, :].rearrange("p (k n) -> p n k", k=GROUP),
                                         ACT.Copy).then_inc(S["w_copied"], 1)

                def down_head(x, b, n, first=False):
                    act.wait_ge(in_d[b], (n + 1) * 16)
                    if not first:
                        act.wait_ge(S["down_done"], x - 1)
                    nc.scalar.activation(hi_d[:, b, :], raw_d[:, b, :], ACT.Copy).then_inc(S["hi_d_ready"], 1)

                def up_head(x, b, n, first=False):
                    act.wait_ge(in_u[b], (n + 1) * 16)
                    if not first:
                        act.wait_ge(S["up_done"], x - 1)
                    nc.scalar.activation(hi_u[:, b, :], raw_u[:, b, :], ACT.Copy).then_inc(S["hi_u_ready"], 1)

                def gelu(x, b, first=False):
                    act.wait_ge(S["down_done"], x + 1)
                    if not first:
                        act.wait_ge(S["g_lo_ready"], x - 1)
                    nc.scalar.activation(gact[:, b, :], psD[:, b, 0:T], ACT.Gelu).then_inc(S["gelu_done"], 1)

                def weighted_head(x, b, first=False):
                    act.wait_ge(S["weighted"], x + 1)
                    if not first:
                        act.wait_ge(S["up_done"], x - 1)
                    nc.scalar.activation(g_hi[:, b, :], gact[:, b, :], ACT.Copy).then_inc(S["g_hi_ready"], 1)

                down_head(0, 0, 0, True)
                down_head(1, 1, 0, True)
                up_head(0, 0, 0, True)
                with act.Fori(0, T // (2 * GROUP)) as i:
                    for g in range(2):
                        to_w(i, g)
                for x in range(2):
                    gelu(x, x, True)
                    down_head(x + 2, x, 1)
                    weighted_head(x, x, True)
                    up_head(x + 1, 1 - x, x, x == 0)
                with act.Fori(1, pairs - 1) as i:
                    for b in range(2):
                        gelu(i * 2 + b, b)
                        down_head(i * 2 + (b + 2), b, i + 1)
                        weighted_head(i * 2 + b, b)
                        up_head(i * 2 + (b + 1), 1 - b, i + b)
                gelu(NE - 2, 0)
                weighted_head(NE - 2, 0)
                up_head(NE - 1, 1, pairs - 1)
                gelu(NE - 1, 1)
                weighted_head(NE - 1, 1)
                act.wait_ge(S["gate_mm"], 1)
                act.wait_ge(S["lo_u_ready"], NE)
                nc.scalar.activation(gate[:, :].rearrange("p (a n) -> p a n", a=2), psW[:, :, :], ACT.Copy).then_inc(S["gate_ready"], 1)

            @block.vector
            def _(dve):
                V = nc.vector

                def one_hots(i, g, first):
                    if not first:
                        dve.wait_ge(S["w_mm"], i * 2 + (g - 1))
                    keys = i2T[:, bass.ds(i * (2 * GROUP) + g * GROUP, GROUP)]
                    V.tensor_tensor(hot2[:, g, :, :], iota[:, :].rearrange("p (a n) -> p a n", a=1).to_broadcast([P, GROUP, NE]),
                                    keys.rearrange("p (a n) -> p a n", n=1).to_broadcast([P, GROUP, NE]),
                                    ALU.is_equal).then_inc(S["hot2_ready"], 1)
                    for k in range(GROUP):
                        t = bass.ds(i * (2 * GROUP) + (g * GROUP + k), 1)
                        ins = V.tensor_scalar(hot1[:, g, k, :], iota[:, :], i1T[:, t], gT[:, t], ALU.is_equal, ALU.mult)
                    ins.then_inc(S["hot1_ready"], 1)

                def down_rest(x, b):
                    dve.wait_ge(S["hi_d_ready"], x + 1)
                    V.tensor_tensor(lo_d[:, b, :], raw_d[:, b, :], hi_d[:, b, :].bitcast(F32), ALU.subtract).then_inc(S["lo_d_ready"], 1)

                def up_rest(x, b):
                    dve.wait_ge(S["hi_u_ready"], x + 1)
                    V.tensor_tensor(lo_u[:, b, :], raw_u[:, b, :], hi_u[:, b, :].bitcast(F32), ALU.subtract).then_inc(S["lo_u_ready"], 1)

                def weigh(x, b):
                    dve.wait_ge(S["gelu_done"], x + 1)
                    key = bass.ds(x, 1)
                    V.tensor_tensor(gact[:, b, :], gact[:, b, :], W[:, key, :].rearrange("p o n -> p (o n)"), ALU.mult).then_inc(S["weighted"], 1)

                def weighted_rest(x, b):
                    dve.wait_ge(S["g_hi_ready"], x + 1)
                    V.tensor_tensor(g_lo[:, b, :], gact[:, b, :], g_hi[:, b, :].bitcast(F32), ALU.subtract).then_inc(S["g_lo_ready"], 1)

                dve.wait_ge(S["in_const"], 32)
                for g in range(2):
                    one_hots(0, g, True)
                with dve.Fori(1, T // (2 * GROUP)) as i:
                    for g in range(2):
                        one_hots(i, g, False)
                down_rest(0, 0)
                down_rest(1, 1)
                dve.wait_ge(S["w_copied"], T // GROUP)
                up_rest(0, 0)
                for x in range(2):
                    weigh(x, x)
                    down_rest(x + 2, x)
                    weighted_rest(x, x)
                    up_rest(x + 1, 1 - x)
                with dve.Fori(1, pairs - 1) as i:
                    for b in range(2):
                        weigh(i * 2 + b, b)
                        down_rest(i * 2 + (b + 2), b)
                        weighted_rest(i * 2 + b, b)
                        up_rest(i * 2 + (b + 1), 1 - b)
                weigh(NE - 2, 0)
                weighted_rest(NE - 2, 0)
                up_rest(NE - 1, 1)
                weigh(NE - 1, 1)
                weighted_rest(NE - 1, 1)
                dve.wait_ge(S["gate_ready"], 1)
                dve.wait_ge(S["up_done"], NE)
                dve.wait_ge(S["in_x"], 16)
                for n in range(4):
                    t, c = divmod(n, 2)
                    c = slice(c * CH, (c + 1) * CH)
                    V.tensor_tensor(prod[:, t, c], psY[:, n, :], gate[:, c], ALU.mult).then_inc(S["prod_done"], 1)
                for n in range(4):
                    t, c = divmod(n, 2)
                    c = slice(c * CH, (c + 1) * CH)
                    dve.wait_ge(S["prod_done"], n + 1)
                    V.tensor_tensor(Xr[:, t, c], Xr[:, t, c], prod[:, t, c], ALU.add).then_inc(S["x_done"], 1)
        clear(nc, S)


def program(nc, inp):
    env = dict(xd=inp["out"], bias_rows=inp["bias_rows"])
    persistent(nc, env)
    prepare(nc, env, inp)
    with nc.Fori(0, DEPTH) as l:
        first_layer(nc, env, l, inp)
    with nc.Fori(0, DEPTH) as l:
        second_mixer(nc, env, l, inp)
        peer(nc, env, l, inp)


def unit_array(w, r0, c0, layout):
    tiles, cols = (4, 512) if layout == "A" else (8, 256)
    cut = w[r0:r0 + tiles * P, c0:c0 + cols]
    return cut.reshape(tiles, P, cols).transpose(1, 0, 2).reshape(P, UNIT)


def columns(v):
    return v.reshape(-1, P).T


def constants():
    f = np.float32
    pos = np.arange(T, dtype=f)

    def angles(theta, half):
        inv = f(theta) ** (-np.arange(half, dtype=f) / f(half))
        return (pos[:, None] * inv[None, :].astype(f)).astype(f)

    ar = angles(10000.0, 128)
    aa = angles(500000.0, 8)
    i, j = np.arange(T)[None, :], np.arange(T)[:, None]
    qi, kj = np.arange(T)[:, None], np.arange(T)[None, :]
    token_rows = lambda a: a.reshape(NT, P, -1).transpose(1, 0, 2).reshape(P, -1)
    parts = dict(
        ident=np.eye(P), cosr=np.cos(ar).T, sinr=np.sin(ar).T,
        mask=token_rows(np.where(np.abs(qi - kj) <= 128, 0.0, NEG)),
        pos=token_rows(np.maximum(i - j, 0)), neg=token_rows(np.maximum(j - i, 0)),
        cosa=token_rows(np.cos(aa)), sina=token_rows(np.sin(aa)),
        iota=np.tile(np.arange(P), (P, 1)), caus=np.triu(np.ones((P, P))))
    out = np.concatenate([parts[k].astype(f) for k in CONSTS], axis=1)
    assert out.shape == (P, CN)
    return np.ascontiguousarray(out)


def first_arrays(x, norm_g, w_in, b_gate, conv_dw, conv_b, conv_ln_g, conv_ln_b, ret_decay, q_norm_g, k_norm_g,
                 attn_sink, w_conv_out, w_ret_out, w_attn_out, w_out):
    weights = dict(w_in=w_in, w_conv_out=w_conv_out, w_ret_out=w_ret_out, w_attn_out=w_attn_out, w_out=w_out)
    ws1 = np.empty((DEPTH * U1, P, UNIT), np.float32)
    for l in range(DEPTH):
        for u, (w, r0, c0, layout) in enumerate(SRC1):
            ws1[l * U1 + u] = unit_array(weights[w][l], r0, c0, layout)
    par = np.empty((DEPTH, P, P1N), np.float32)
    for l in range(DEPTH):
        rows = dict(norm_g=columns(norm_g[l]), dw=conv_dw[l].T.reshape(KT, P, TAPS).transpose(1, 0, 2).reshape(P, -1),
                    db=columns(conv_b[l]), ln_g=columns(conv_ln_g[l]), ln_b=columns(conv_ln_b[l]),
                    qg=np.tile(q_norm_g[l], (P, 1)), kg=np.tile(k_norm_g[l], (P, 1)), sink=np.tile(attn_sink[l], (P, 1)),
                    decay=np.tile(ret_decay[l].reshape(-1), (P, 1)))
        for k, (a, n) in P1OFF.items():
            par[l, :, a:a + n] = rows[k]
    bgate = np.ascontiguousarray(np.broadcast_to(b_gate.reshape(DEPTH * 3, 1, D), (DEPTH * 3, P, D)))
    return dict(x=np.ascontiguousarray(x.reshape(NT, P, D).transpose(1, 0, 2)), consts=constants(), par1=par, bgate=bgate, ws1=ws1)


def second_arrays(c_2, rel_bias_2, w_ada_2, b_ada_2, norm1_g_2, norm2_g_2, w_in_2, q_norm_g_2, k_norm_g_2, attn_sink_2,
                  conv_w_2, sgu_w_2, sgu_b_2, out_norm_g_2, w_out_2, peer_wq_2, peer_sub_keys_2, peer_down_2, peer_up_2):
    f = np.float32
    cols = np.r_[0:768, 1536:2048, 1280:1536, 1024:1280, 768:1024]
    weights = dict(w_in_2=w_in_2[:, :, cols], w_out_2=w_out_2, peer_wq_2=peer_wq_2)
    ws2 = np.empty((DEPTH * U2, P, UNIT), f)
    ada = np.empty((DEPTH * ADA_U, P, UNIT), f)
    par = np.empty((DEPTH, P, P2N), f)
    for l in range(DEPTH):
        for u, (w, r0, c0, layout) in enumerate(SRC2):
            ws2[l * U2 + u] = unit_array(weights[w][l], r0, c0, layout)
        for u in range(ADA_U):
            ada[l * ADA_U + u] = unit_array(w_ada_2[l], 0, 256 * u, "B")
        rows = dict(norm1_g=columns(norm1_g_2[l]), norm2_g=columns(norm2_g_2[l]), gain=columns(out_norm_g_2[l]),
                    conv_w=conv_w_2[l].T.reshape(2, P, 3).transpose(1, 0, 2).reshape(P, 6), sgu_b=sgu_b_2[l].T,
                    qg=np.tile(q_norm_g_2[l], (P, 1)), kg=np.tile(k_norm_g_2[l], (P, 1)), sink=np.tile(attn_sink_2[l], (P, 1)))
        for k, (a, n) in P2OFF.items():
            par[l, :, a:a + n] = rows[k]
    dist = 255 - np.arange(BIAS_N)
    d = np.maximum(dist, 1).astype(f)
    ratio = (np.log(d / f(16)) / f(np.log(128 / 16))).astype(f)
    large = np.minimum(16 + (ratio * f(16)).astype(np.int32), 31)
    bucket = np.where(dist < 16, dist, large)
    valid = (dist >= 0) & (dist < 128)
    pick = np.zeros((33, BIAS_N), f)
    for u in range(BIAS_N):
        pick[bucket[u] if valid[u] else 32, u] = 1.0
    return dict(c=np.ascontiguousarray(columns(c_2[0])), b_ada=np.concatenate([columns(b_ada_2[l]) for l in range(DEPTH)], axis=1),
                rel=rel_bias_2, pick=pick, ada=ada, par2=par, ws2=ws2,
                sgw=np.ascontiguousarray(sgu_w_2.transpose(0, 3, 1, 2).reshape(DEPTH, P, 4 * P)),
                keys=np.ascontiguousarray(peer_sub_keys_2.transpose(0, 4, 1, 2, 3).reshape(DEPTH, P, 16 * NE)),
                down=np.ascontiguousarray(peer_down_2.reshape(DEPTH, NE, NE, KT, P).transpose(0, 1, 4, 3, 2).reshape(DEPTH * NE, P, D)),
                up=peer_up_2.reshape(DEPTH * NE, NE, D))


def kernel(x, norm_g, w_in, b_gate, conv_dw, conv_b, conv_ln_g, conv_ln_b, ret_decay, q_norm_g, k_norm_g, attn_sink,
           w_conv_out, w_ret_out, w_attn_out, w_out, c_2, rel_bias_2, w_ada_2, b_ada_2, norm1_g_2, norm2_g_2, w_in_2,
           q_norm_g_2, k_norm_g_2, attn_sink_2, conv_w_2, sgu_w_2, sgu_b_2, out_norm_g_2, w_out_2, peer_wq_2,
           peer_sub_keys_2, peer_down_2, peer_up_2):
    import concourse.bacc as bacc
    from concourse.bass_utils import run_bass_kernel_spmd

    arrays = first_arrays(x, norm_g, w_in, b_gate, conv_dw, conv_b, conv_ln_g, conv_ln_b, ret_decay, q_norm_g, k_norm_g,
                          attn_sink, w_conv_out, w_ret_out, w_attn_out, w_out)
    arrays.update(second_arrays(c_2, rel_bias_2, w_ada_2, b_ada_2, norm1_g_2, norm2_g_2, w_in_2, q_norm_g_2, k_norm_g_2,
                                attn_sink_2, conv_w_2, sgu_w_2, sgu_b_2, out_norm_g_2, w_out_2, peer_wq_2,
                                peer_sub_keys_2, peer_down_2, peer_up_2))
    arrays = {name: np.ascontiguousarray(a) for name, a in arrays.items()}
    nc = bacc.Bacc("TRN2", target_bir_lowering=False, num_devices=1)
    inp = {name: nc.dram_tensor(name, a.shape, mybir.dt.from_np(a.dtype), kind="ExternalInput").ap() for name, a in arrays.items()}
    inp["bias_rows"] = nc.dram_tensor("bias_rows", (P, H2, BIAS_N), F32, kind="Internal").ap()
    inp["out"] = nc.dram_tensor("out", (P, NT, D), F32, kind="ExternalOutput").ap()
    program(nc, inp)
    r = run_bass_kernel_spmd(nc, [arrays], core_ids=[0])
    return np.ascontiguousarray(r.results[0]["out"].transpose(1, 0, 2)).reshape(1, T, D)
```
